# Optimizing a Trainium2 kernel written in Bass

```python
import math
import jax
import jax.numpy as jnp
from jax import lax
import numpy as np
import jax, jax.numpy as jnp

D_MODEL = 1024
BATCH = 1
SEQ = 512
DEPTH = 4

N_MIXERS = 3
N_A = (DEPTH + 2) // N_MIXERS
N_B = (DEPTH + 1) // N_MIXERS
N_C = DEPTH // N_MIXERS

DA_HEADS = 8
DA_HEAD_DIM = 64
DA_QK = 2 * DA_HEADS * DA_HEAD_DIM
DA_V = DA_HEADS * 2 * DA_HEAD_DIM
HG_EXPAND = 128
HG_HEADS = D_MODEL // HG_EXPAND
HG_KDIM = HG_EXPAND
HG_VDIM = D_MODEL // HG_HEADS
HG_FDIM = HG_HEADS * HG_KDIM
HG_CHUNK = 64
SW_Q_HEADS = 16
SW_KV_HEADS = 2
SW_HEAD_DIM = 64
SW_GROUP = SW_Q_HEADS // SW_KV_HEADS
SW_WINDOW = 128
SW_IN = SW_Q_HEADS * SW_HEAD_DIM + 2 * SW_KV_HEADS * SW_HEAD_DIM
N_BUCKETS = 32
MAX_DISTANCE = 128
N_BIAS_HEADS = 16
BLOCK = 128
D_FF = 4 * D_MODEL
PLE_DIM = 256
ALPHA = (2 * DEPTH) ** 0.25
BETA = (8 * DEPTH) ** -0.25
LN_EPS = 1e-5
RMS_EPS = 1e-6


def layer_norm(x, g, b):
    x32 = x.astype(jnp.float32)
    mu = jnp.mean(x32, axis=-1, keepdims=True)
    var = jnp.mean(jnp.square(x32 - mu), axis=-1, keepdims=True)
    y = (x32 - mu) * lax.rsqrt(var + LN_EPS) * g.astype(jnp.float32) + b.astype(jnp.float32)
    return y.astype(x.dtype)

def rms_norm(x, g):
    x32 = x.astype(jnp.float32)
    y = x32 * lax.rsqrt(jnp.mean(jnp.square(x32), axis=-1, keepdims=True) + RMS_EPS)
    return (y * g.astype(jnp.float32)).astype(x.dtype)

def t5_bucket(rel):
    n = jnp.maximum(rel, 0)
    max_exact = N_BUCKETS // 2
    nf = jnp.maximum(n, 1).astype(jnp.float32)
    large = max_exact + (jnp.log(nf / max_exact) / math.log(MAX_DISTANCE / max_exact)
                         * (N_BUCKETS - max_exact)).astype(jnp.int32)
    large = jnp.minimum(large, N_BUCKETS - 1)
    return jnp.where(n < max_exact, n, large)

def diff_attention(h, w_in, lam, subln, w_out, rel_bias, layer_idx):
    B, S, _ = h.shape
    H, d = DA_HEADS, DA_HEAD_DIM
    q, k, v = jnp.split(h @ w_in, [DA_QK, 2 * DA_QK], axis=-1)
    q = q.reshape(B, S, 2 * H, d).transpose(0, 2, 1, 3) * (d ** -0.5)
    k = k.reshape(B, S, 2 * H, d).transpose(0, 2, 1, 3)
    v = v.reshape(B, S, H, 2 * d).transpose(0, 2, 1, 3)
    lam_init = 0.8 - 0.6 * math.exp(-0.3 * layer_idx)
    lam32 = lam.astype(jnp.float32)
    lam_full = jnp.exp(jnp.sum(lam32[0] * lam32[1])) - jnp.exp(jnp.sum(lam32[2] * lam32[3])) + lam_init
    pos = jnp.arange(S, dtype=jnp.int32)
    outs = []
    for blk in range(S // BLOCK):
        qs = blk * BLOCK
        ke = qs + BLOCK
        s = jnp.einsum('bmqd,bmkd->bmqk', q[:, :, qs:ke], k[:, :, :ke]).astype(jnp.float32)
        rel = pos[qs:ke, None] - pos[None, :ke]
        bias = rel_bias[t5_bucket(rel)].astype(jnp.float32).transpose(2, 0, 1)
        s = jnp.where(rel >= 0, s + bias, -jnp.inf)
        a = jax.nn.softmax(s, axis=-1).reshape(B, H, 2, BLOCK, ke)
        a = a[:, :, 0] - lam_full * a[:, :, 1]
        outs.append(jnp.einsum('bhqk,bhkv->bhqv', a.astype(v.dtype), v[:, :, :ke]))
    o = jnp.concatenate(outs, axis=2)
    o = rms_norm(o, subln) * (1.0 - lam_init)
    o = o.transpose(0, 2, 1, 3).reshape(B, S, DA_V)
    return o @ w_out

def hgrn2(h, w_in, gnorm, w_out, lower_bound):
    B, S, _ = h.shape
    H, dk, dv, C = HG_HEADS, HG_KDIM, HG_VDIM, HG_CHUNK
    q, f, i, g = jnp.split(h @ w_in, 4, axis=-1)
    q = jax.nn.silu(q.astype(jnp.float32))
    lb = lower_bound.astype(jnp.float32)
    f = lb + (1.0 - lb) * jax.nn.sigmoid(f.astype(jnp.float32))
    logf = jnp.log(f)
    kin = 1.0 - f

    def to_chunks(t, dim):
        return t.reshape(B, S // C, C, H, dim).transpose(1, 0, 3, 2, 4)

    qc, kc, gc = to_chunks(q, dk), to_chunks(kin, dk), to_chunks(logf, dk)
    vc = to_chunks(i.astype(jnp.float32), dv)
    causal = jnp.tril(jnp.ones((C, C), dtype=bool))

    def step(state, inp):
        q_, k_, v_, g_ = inp
        G = jnp.cumsum(g_, axis=2)
        G_last = G[:, :, -1:, :]
        o_inter = jnp.einsum('bhtk,bhkv->bhtv', q_ * jnp.exp(G), state)
        diff = G[:, :, :, None, :] - G[:, :, None, :, :]
        decay = jnp.exp(jnp.where(causal[:, :, None], diff, -jnp.inf))
        A = jnp.einsum('bhtk,bhsk,bhtsk->bhts', q_, k_, decay)
        o = o_inter + jnp.einsum('bhts,bhsv->bhtv', A, v_)
        new_state = (jnp.exp(G_last[:, :, 0, :])[..., None] * state
                     + jnp.einsum('bhsk,bhsv->bhkv', k_ * jnp.exp(G_last - G), v_))
        return new_state, o

    s0 = jnp.zeros((B, H, dk, dv), jnp.float32)
    _, o = lax.scan(step, s0, (qc, kc, vc, gc))
    o = o.transpose(1, 0, 3, 2, 4).reshape(B, S, H, dv)
    o = rms_norm(o, gnorm) * jax.nn.silu(g.astype(jnp.float32).reshape(B, S, H, dv))
    o = o.reshape(B, S, H * dv).astype(h.dtype)
    return o @ w_out

def swa_sink_attention(h, w_in, sinks, w_out, rel_bias):
    B, S, _ = h.shape
    Hq, Hk, G, d, W = SW_Q_HEADS, SW_KV_HEADS, SW_GROUP, SW_HEAD_DIM, BLOCK
    NB = S // W
    q, k, v = jnp.split(h @ w_in, [Hq * d, Hq * d + Hk * d], axis=-1)
    q = q.reshape(B, NB, W, Hk, G, d) * (d ** -0.5)
    k = k.reshape(B, NB, W, Hk, d)
    v = v.reshape(B, NB, W, Hk, d)

    def prev_block(t):
        return jnp.concatenate([jnp.zeros_like(t[:, :1]), t[:, :-1]], axis=1)

    kb = jnp.concatenate([prev_block(k), k], axis=2)
    vb = jnp.concatenate([prev_block(v), v], axis=2)
    s = jnp.einsum('bnqhgd,bnkhd->bnhgqk', q, kb).astype(jnp.float32)
    qi = jnp.arange(W, dtype=jnp.int32)[:, None]
    kj = jnp.arange(2 * W, dtype=jnp.int32)[None, :]
    rel = qi + W - kj
    bias = rel_bias[t5_bucket(rel)].astype(jnp.float32).transpose(2, 0, 1).reshape(Hk, G, W, 2 * W)
    in_window = (rel >= 0) & (rel < SW_WINDOW)
    key_valid = (jnp.arange(NB, dtype=jnp.int32)[:, None, None] * W + kj[None] - W) >= 0
    mask = in_window[None] & key_valid
    s = jnp.where(mask[None, :, None, None], s + bias, -jnp.inf)
    sink = sinks.astype(jnp.float32).reshape(Hk, G)[None, None, :, :, None, None]
    m = jnp.maximum(jnp.max(s, axis=-1, keepdims=True), sink)
    e = jnp.exp(s - m)
    a = e / (jnp.sum(e, axis=-1, keepdims=True) + jnp.exp(sink - m))
    o = jnp.einsum('bnhgqk,bnkhd->bnqhgd', a.astype(vb.dtype), vb).reshape(B, S, Hq * d)
    return o @ w_out

def first_inputs(seed: int = 0) -> dict:
    key = jax.random.key(seed)
    ks = jax.random.split(key, 24)
    f32 = jnp.float32
    D = D_MODEL

    def nrm(k, shape, scale):
        return jax.random.normal(k, shape, f32) * scale

    return {
        "x": nrm(ks[0], (BATCH, SEQ, D), 1.0),
        "p": nrm(ks[1], (DEPTH, BATCH, SEQ, PLE_DIM), 1.0),
        "rel_bias": nrm(ks[2], (N_BUCKETS, N_BIAS_HEADS), 0.5),
        "hg_lower_bound": nrm(ks[3], (DEPTH, HG_FDIM), 0.1),
        "da_w_in": nrm(ks[4], (N_A, D, 2 * DA_QK + DA_V), D ** -0.5),
        "da_lambda": nrm(ks[5], (N_A, 4, DA_HEAD_DIM), 0.1),
        "da_subln": 1.0 + nrm(ks[6], (N_A, 2 * DA_HEAD_DIM), 0.02),
        "da_w_out": nrm(ks[7], (N_A, DA_V, D), DA_V ** -0.5 * BETA),
        "hg_w_in": nrm(ks[8], (N_B, D, 2 * HG_FDIM + 2 * D), D ** -0.5),
        "hg_gnorm": 1.0 + nrm(ks[9], (N_B, HG_VDIM), 0.02),
        "hg_w_out": nrm(ks[10], (N_B, D, D), D ** -0.5 * BETA),
        "sw_w_in": nrm(ks[11], (N_C, D, SW_IN), D ** -0.5),
        "sw_sinks": nrm(ks[12], (N_C, SW_Q_HEADS), 0.5),
        "sw_w_out": nrm(ks[13], (N_C, SW_Q_HEADS * SW_HEAD_DIM, D), (SW_Q_HEADS * SW_HEAD_DIM) ** -0.5 * BETA),
        "ln_g": 1.0 + nrm(ks[14], (DEPTH, 2, D), 0.02),
        "ln_b": nrm(ks[15], (DEPTH, 2, D), 0.02),
        "w_up": nrm(ks[16], (DEPTH, D, D_FF), D ** -0.5),
        "w_down": nrm(ks[17], (DEPTH, D_FF, D), D_FF ** -0.5 * BETA),
        "w_ple": nrm(ks[18], (DEPTH, PLE_DIM, D), PLE_DIM ** -0.5 * 0.5),
        "w_ple_gate": nrm(ks[19], (DEPTH, D, D), D ** -0.5),
    }

def first_block(x, p, rel_bias, hg_lower_bound, da_w_in, da_lambda, da_subln, da_w_out,
              hg_w_in, hg_gnorm, hg_w_out, sw_w_in, sw_sinks, sw_w_out,
              ln_g, ln_b, w_up, w_down, w_ple, w_ple_gate):
    lb_sm = jax.nn.softmax(hg_lower_bound.astype(jnp.float32), axis=0)
    lb_all = jnp.cumsum(lb_sm, axis=0) - lb_sm[0]
    h = x
    for i in range(DEPTH):
        kind, j = i % N_MIXERS, i // N_MIXERS
        if kind == 0:
            y = diff_attention(h, da_w_in[j], da_lambda[j], da_subln[j], da_w_out[j], rel_bias, i)
        elif kind == 1:
            y = hgrn2(h, hg_w_in[j], hg_gnorm[j], hg_w_out[j], lb_all[i])
        else:
            y = swa_sink_attention(h, sw_w_in[j], sw_sinks[j], sw_w_out[j], rel_bias)
        h = layer_norm(ALPHA * h + y, ln_g[i, 0], ln_b[i, 0])
        u = jnp.square(jax.nn.relu(h @ w_up[i])) @ w_down[i]
        h = layer_norm(ALPHA * h + u, ln_g[i, 1], ln_b[i, 1])
        h = h + jax.nn.sigmoid(h @ w_ple_gate[i]) * (p[i] @ w_ple[i])
    return h


DEPTH_2 = 1

CHUNK = 64
RET_HEADS = 4
RET_DK = 128
RET_DV = 256
RET_QK_WIDTH = RET_HEADS * RET_DK
RET_V_WIDTH = RET_HEADS * RET_DV
LRU_WIDTH = 1024
LRU_BLOCKS = 4
LRU_BLOCK = LRU_WIDTH // LRU_BLOCKS
LRU_CONV = 4
LRU_C = 8.0
LRU_MIN_RAD = 0.9
LRU_MAX_RAD = 0.999
D_FF_2 = 3 * D_MODEL
FFN_CONV = 3
ROPE_BASE = 10000.0
GN_EPS = 1e-6

IN_SIZES = (RET_QK_WIDTH, RET_QK_WIDTH, RET_V_WIDTH, RET_V_WIDTH,
            LRU_WIDTH, LRU_WIDTH, D_MODEL, D_MODEL)
D_IN = sum(IN_SIZES)
SPLIT_POINTS = tuple(sum(IN_SIZES[:i + 1]) for i in range(len(IN_SIZES) - 1))


def rms_norm_2(x, w):
    x32 = x.astype(jnp.float32)
    y = x32 * lax.rsqrt(jnp.mean(x32 * x32, axis=-1, keepdims=True) + RMS_EPS)
    return (y * w.astype(jnp.float32)).astype(x.dtype)

def causal_depthwise_conv(x, w, b):
    k_width, channels = w.shape
    y = lax.conv_general_dilated(
        x, w[:, None, :].astype(x.dtype), window_strides=(1,),
        padding=[(k_width - 1, 0)], dimension_numbers=("NWC", "WIO", "NWC"),
        feature_group_count=channels)
    return y + b.astype(x.dtype)

def rotary(x, positions):
    half = x.shape[-1] // 2
    inv_freq = ROPE_BASE ** (-jnp.arange(half, dtype=jnp.float32) / half)
    ang = positions.astype(jnp.float32)[..., None] * inv_freq
    cos = jnp.cos(ang)[:, :, None, :]
    sin = jnp.sin(ang)[:, :, None, :]
    x32 = x.astype(jnp.float32)
    x1, x2 = x32[..., :half], x32[..., half:]
    return jnp.concatenate([x1 * cos - x2 * sin, x1 * sin + x2 * cos], axis=-1).astype(x.dtype)

def chunkwise_retention(q, k, v):
    bsz, seq, heads, dk = q.shape
    dv = v.shape[-1]
    n_chunks = seq // CHUNK
    log_gamma = jnp.log1p(-jnp.power(2.0, -5.0 - jnp.arange(heads, dtype=jnp.float32)))
    idx = jnp.arange(CHUNK, dtype=jnp.float32)
    dist = jnp.abs(idx[:, None] - idx[None, :])
    intra_decay = jnp.exp(log_gamma[:, None, None] * dist)
    q_decay = jnp.exp(log_gamma[:, None] * (idx + 1.0))
    k_decay = jnp.exp(log_gamma[:, None] * (CHUNK - 1.0 - idx))
    chunk_decay = jnp.exp(log_gamma * CHUNK)

    def to_chunks(t):
        return t.astype(jnp.float32).reshape(bsz, n_chunks, CHUNK, heads, -1).transpose(1, 0, 3, 2, 4)

    qc, kc, vc = to_chunks(q), to_chunks(k), to_chunks(v)

    def step(state, inp):
        qi, ki, vi = inp
        scores = jnp.einsum("bhid,bhjd->bhij", qi, ki) * intra_decay
        out = (jnp.einsum("bhij,bhjv->bhiv", scores, vi)
               + jnp.einsum("bhid,bhdv->bhiv", qi * q_decay[:, :, None], state))
        state = (state * chunk_decay[:, None, None]
                 + jnp.einsum("bhjd,bhjv->bhdv", ki * k_decay[:, :, None], vi))
        return state, out

    state0 = jnp.zeros((bsz, heads, dk, dv), jnp.float32)
    _, out = lax.scan(step, state0, (qc, kc, vc))
    return out.transpose(1, 0, 3, 2, 4).reshape(bsz, seq, heads, dv)

def head_group_norm(o, w):
    bsz, seq, heads, dv = o.shape
    mu = jnp.mean(o, axis=-1, keepdims=True)
    var = jnp.mean(jnp.square(o - mu), axis=-1, keepdims=True)
    y = (o - mu) * lax.rsqrt(var + GN_EPS)
    return y.reshape(bsz, seq, heads * dv) * w.astype(jnp.float32)

def _linear_recurrence_combine(e1, e2):
    a1, b1 = e1
    a2, b2 = e2
    return a1 * a2, a2 * b1 + b2

def rg_lru(x, w_r, b_r, w_i, b_i, lam):
    bsz, seq, width = x.shape
    x32 = x.astype(jnp.float32)
    xb = x32.reshape(bsz, seq, LRU_BLOCKS, LRU_BLOCK)
    r = jax.nn.sigmoid(jnp.einsum("bsni,nij->bsnj", xb, w_r.astype(jnp.float32))
                       + b_r.astype(jnp.float32)).reshape(bsz, seq, width)
    i = jax.nn.sigmoid(jnp.einsum("bsni,nij->bsnj", xb, w_i.astype(jnp.float32))
                       + b_i.astype(jnp.float32)).reshape(bsz, seq, width)
    log_a = -LRU_C * r * jax.nn.softplus(-lam.astype(jnp.float32))
    a = jnp.exp(log_a)
    b = jnp.sqrt(-jnp.expm1(2.0 * log_a)) * (i * x32)
    _, h = lax.associative_scan(_linear_recurrence_combine, (a, b), axis=1)
    return h

def second_inputs(seed: int = 0) -> dict:
    key = jax.random.key(seed)
    ks = jax.random.split(key, 24)

    def nrm(k, shape, scale):
        return jax.random.normal(k, shape, jnp.float32) * scale

    def gain(k, shape):
        return 1.0 + 0.02 * jax.random.normal(k, shape, jnp.float32)

    x = jax.random.normal(ks[0], (BATCH, SEQ, D_MODEL), jnp.float32)
    start = jax.random.randint(ks[1], (BATCH, 1), 0, 64) * CHUNK
    positions = (start + jnp.arange(SEQ)[None, :]).astype(jnp.int32)

    u = jax.random.uniform(ks[12], (DEPTH_2, LRU_WIDTH), jnp.float32,
                           LRU_MIN_RAD ** 2, LRU_MAX_RAD ** 2)
    a0 = jnp.sqrt(u)
    lru_lambda = jnp.log(a0) - jnp.log1p(-a0)

    return {
        "x": x,
        "positions": positions,
        "norm1_w": gain(ks[2], (DEPTH_2, D_MODEL)),
        "w_in": nrm(ks[3], (DEPTH_2, D_MODEL, D_IN), D_MODEL ** -0.5),
        "merge_gate_b": nrm(ks[4], (DEPTH_2, 2, D_MODEL), 0.02),
        "ret_gn_w": gain(ks[5], (DEPTH_2, RET_V_WIDTH)),
        "w_ret_o": nrm(ks[6], (DEPTH_2, RET_V_WIDTH, D_MODEL), RET_V_WIDTH ** -0.5),
        "lru_conv_w": nrm(ks[7], (DEPTH_2, LRU_CONV, LRU_WIDTH), LRU_CONV ** -0.5),
        "lru_conv_b": nrm(ks[8], (DEPTH_2, LRU_WIDTH), 0.02),
        "lru_w_r": nrm(ks[9], (DEPTH_2, LRU_BLOCKS, LRU_BLOCK, LRU_BLOCK), LRU_BLOCK ** -0.5),
        "lru_b_r": nrm(ks[10], (DEPTH_2, LRU_BLOCKS, LRU_BLOCK), 0.02),
        "lru_w_i": nrm(ks[11], (DEPTH_2, LRU_BLOCKS, LRU_BLOCK, LRU_BLOCK), LRU_BLOCK ** -0.5),
        "lru_b_i": nrm(ks[13], (DEPTH_2, LRU_BLOCKS, LRU_BLOCK), 0.02),
        "lru_lambda": lru_lambda,
        "w_lru_o": nrm(ks[14], (DEPTH_2, LRU_WIDTH, D_MODEL), LRU_WIDTH ** -0.5),
        "w_out": nrm(ks[15], (DEPTH_2, D_MODEL, D_MODEL), D_MODEL ** -0.5),
        "norm2_w": gain(ks[16], (DEPTH_2, D_MODEL)),
        "ffn_w_up": nrm(ks[17], (DEPTH_2, D_MODEL, 2 * D_FF_2), D_MODEL ** -0.5),
        "ffn_conv_w": nrm(ks[18], (DEPTH_2, FFN_CONV, D_FF_2), FFN_CONV ** -0.5),
        "ffn_conv_b": nrm(ks[19], (DEPTH_2, D_FF_2), 0.02),
        "ffn_w_down": nrm(ks[20], (DEPTH_2, D_FF_2, D_MODEL), D_FF_2 ** -0.5),
        "norm_f_w": gain(ks[21], (D_MODEL,)),
    }

def second_block(x, positions, norm1_w, w_in, merge_gate_b, ret_gn_w, w_ret_o,
              lru_conv_w, lru_conv_b, lru_w_r, lru_b_r, lru_w_i, lru_b_i, lru_lambda,
              w_lru_o, w_out, norm2_w, ffn_w_up, ffn_conv_w, ffn_conv_b, ffn_w_down,
              norm_f_w):
    bsz, seq, _ = x.shape
    for l in range(DEPTH_2):
        h = rms_norm_2(x, norm1_w[l])
        proj = h @ w_in[l]
        q, k, v, g_ret, x_lru, y_lru, gate_ret, gate_lru = jnp.split(proj, SPLIT_POINTS, axis=-1)

        q = rotary(q.reshape(bsz, seq, RET_HEADS, RET_DK), positions)
        k = rotary(k.reshape(bsz, seq, RET_HEADS, RET_DK), positions) * (RET_DK ** -0.5)
        o = chunkwise_retention(q, k, v.reshape(bsz, seq, RET_HEADS, RET_DV))
        o = head_group_norm(o, ret_gn_w[l])
        y_a = (o * jax.nn.silu(g_ret.astype(jnp.float32))).astype(x.dtype) @ w_ret_o[l]

        xc = causal_depthwise_conv(x_lru, lru_conv_w[l], lru_conv_b[l])
        hl = rg_lru(xc, lru_w_r[l], lru_b_r[l], lru_w_i[l], lru_b_i[l], lru_lambda[l])
        y_b = (hl * jax.nn.gelu(y_lru.astype(jnp.float32))).astype(x.dtype) @ w_lru_o[l]

        mix = (jax.nn.sigmoid(gate_ret + merge_gate_b[l, 0]) * y_a
               + jax.nn.sigmoid(gate_lru + merge_gate_b[l, 1]) * y_b)
        x = x + mix @ w_out[l]

        h = rms_norm_2(x, norm2_w[l])
        up = h @ ffn_w_up[l]
        gate, val = jnp.split(up, [D_FF_2], axis=-1)
        gate = causal_depthwise_conv(gate, ffn_conv_w[l], ffn_conv_b[l])
        x = x + (jax.nn.gelu(gate) * val) @ ffn_w_down[l]
    return rms_norm_2(x, norm_f_w)


def setup_inputs(seed=0):
    out = dict(first_inputs(seed))
    for name, value in second_inputs(seed + 1).items():
        if name != "x":
            out[name + "_2"] = value
    return out


def reference(
    x, p, rel_bias, hg_lower_bound, da_w_in, da_lambda, da_subln, da_w_out, hg_w_in, hg_gnorm,
    hg_w_out, sw_w_in, sw_sinks, sw_w_out, ln_g, ln_b, w_up, w_down, w_ple, w_ple_gate,
    positions_2, norm1_w_2, w_in_2, merge_gate_b_2, ret_gn_w_2, w_ret_o_2, lru_conv_w_2,
    lru_conv_b_2, lru_w_r_2, lru_b_r_2, lru_w_i_2, lru_b_i_2, lru_lambda_2, w_lru_o_2, w_out_2,
    norm2_w_2, ffn_w_up_2, ffn_conv_w_2, ffn_conv_b_2, ffn_w_down_2, norm_f_w_2,
):
    x = first_block(
        x, p, rel_bias, hg_lower_bound, da_w_in, da_lambda, da_subln, da_w_out, hg_w_in,
        hg_gnorm, hg_w_out, sw_w_in, sw_sinks, sw_w_out, ln_g, ln_b, w_up, w_down, w_ple,
        w_ple_gate,
    )
    return second_block(
        x, positions_2, norm1_w_2, w_in_2, merge_gate_b_2, ret_gn_w_2, w_ret_o_2, lru_conv_w_2,
        lru_conv_b_2, lru_w_r_2, lru_b_r_2, lru_w_i_2, lru_b_i_2, lru_lambda_2, w_lru_o_2,
        w_out_2, norm2_w_2, ffn_w_up_2, ffn_conv_w_2, ffn_conv_b_2, ffn_w_down_2, norm_f_w_2,
    )


_drawn_inputs = setup_inputs


def setup_inputs(seed=0):
    import zlib

    import numpy as np

    out = dict(_drawn_inputs(seed))
    spreads = {}
    factors = {'hg_lower_bound': 8.0,
     'da_subln': 8.0,
     'hg_gnorm': 8.0,
     'sw_sinks': 8.0,
     'norm1_w_2': 3.611,
     'merge_gate_b_2': 8.0,
     'ret_gn_w_2': 22.941,
     'lru_conv_b_2': 9.074,
     'lru_b_r_2': 40.6,
     'lru_b_i_2': 27.887,
     'norm2_w_2': 12.755,
     'ffn_conv_b_2': 18.694,
     'norm_f_w_2': 8.097}
    for name, (base, spread) in spreads.items():
        noise = np.random.default_rng([zlib.crc32(name.encode()), seed]).standard_normal(out[name].shape)
        drawn = base * np.exp(spread * noise) if base else spread * noise
        out[name] = jnp.asarray(drawn.astype(out[name].dtype))
    for name, factor in factors.items():
        out[name] = (out[name] * factor).astype(out[name].dtype)
    return out
```

```python
import math
from contextlib import ExitStack

import numpy as np

import concourse.bass as bass
from concourse import mybir

F32 = mybir.dt.float32
F32R = mybir.dt.float32r
I32 = mybir.dt.int32
ALU = mybir.AluOpType
ACT = mybir.ActivationFunctionType

P = 128
S = 512
D = 1024
KT = D // P
NL = 4
ALPHA = (2 * NL) ** 0.25
LN_EPS = 1e-5
RMS_EPS = 1e-6
NEG = -1.0e30
N_BUCKETS = 32
MAX_DISTANCE = 128
RET_HEADS = 4
LAM_INIT = [0.8 - 0.6 * math.exp(-0.3 * i) for i in (0, 3)]



class Plan:

    def __init__(self):
        self.slabs = []
        self.unit_rel = []
        self.unit_slab = []
        self.last_unit = []
        self.at = {}

    def stage(self, name, slabs, rels, order=None):
        s0, u0 = len(self.slabs), len(self.unit_rel)
        self.at[name] = (s0, u0)
        order = order or list(range(len(slabs)))
        self.slabs += slabs
        self.last_unit += [0] * len(slabs)
        for j, s in enumerate(order):
            self.unit_rel.append(rels[j % len(rels)])
            self.unit_slab.append(s0 + s)
            self.last_unit[s0 + s] = u0 + j

    def released(self, unit):
        e = self.unit_rel[unit]
        return e, sum(r == e for r in self.unit_rel[:unit + 1])


def make_plan():
    pl = Plan()
    for layer in range(NL):
        kind, j = layer % 3, layer // 3
        if kind == 0:
            pl.stage(f"mix{layer}", [("da_w_in", j, 0, c + g * 256) for g in range(4) for c in (0, D, 2 * D)], ["act"])
            out = ("da_w_out", j)
        elif kind == 1:
            pl.stage(f"mix{layer}", [("hg_w_in", 0, 0, c + g * 256) for g in range(4) for c in (D, 0, 2 * D, 3 * D)], ["act"])
            out = ("hg_w_out", 0)
        else:
            pl.stage(f"mix{layer}", [("sw_w_in", 0, 0, D)] + [("sw_w_in", 0, 0, g * 256) for g in range(4)], ["act"])
            out = ("sw_w_out", 0)
        pl.stage(f"out{layer}", [(*out, 0, n * 256) for n in range(4)], ["dve"])
        pl.stage(f"ffn{layer}", [x for q in range(4) for x in
                 [("w_up", layer, 0, q * D + n * 256) for n in range(4)] +
                 [("w_down", layer, q * D, n * 256) for n in range(4)]], ["dve"])
        pl.stage(f"ple{layer}", [("w_ple", layer, -1, 0)], ["act"], [0] * 4)
        pl.stage(f"gate{layer}", [("w_ple_gate", layer, 0, n * 256) for n in range(4)], ["act"])
    w = lambda c: ("w_in_2", 0, 0, c)
    pl.stage("ret", [w(c) for g in range(2) for c in
             (g * 256, 512 + g * 256, 1024 + g * 512, 1280 + g * 512, 2048 + g * 512, 2304 + g * 512)], ["act"])
    pl.stage("gret", [w(5120 + n * 256) for n in range(4)], ["act"])
    pl.stage("reto", [("w_ret_o_2", 0, 0, n * 256) for n in range(4)], ["dve"])
    pl.stage("xlru", [w(3072 + n * 256) for n in range(4)], ["dve"])
    gate, both = (lambda n: w(6144 + n * 256)), (lambda n: ("lru_w_r_2", 0, -2, n))
    pl.stage("lru", [gate(0), both(0), gate(1), gate(2), both(1), gate(3)], ["act"], [0, 1, 1, 2, 1, 1, 3, 4, 4, 5, 4, 4])
    pl.stage("ylru", [w(4096 + n * 256) for n in range(4)], ["act"])
    pl.stage("lruo", [("w_lru_o_2", 0, 0, n * 256) for n in range(4)], ["dve"])
    pl.stage("wout", [("w_out_2", 0, 0, n * 256) for n in range(4)], ["dve"])
    pl.stage("ffnb", [x for q in range(3) for x in
             [("ffn_w_up_2", 0, 0, h * 3 * D + q * D + n * 256) for n in range(4) for h in range(2)] +
             [("ffn_w_down_2", 0, q * D, n * 256) for n in range(4)]], ["dve"])
    return pl


PLAN = make_plan()
N_SLABS = len(PLAN.slabs)

X_GEN = {}
G_GEN = {}
for _l in range(NL):
    G_GEN[f"in{_l}"] = 5 * _l
    G_GEN[f"ffn{_l}"] = 5 * _l + 1
    X_GEN[f"mix{_l}"], X_GEN[f"ln1{_l}"], X_GEN[f"ln2{_l}"] = 3 * _l, 3 * _l + 1, 3 * _l + 2
G_GEN["in4"], G_GEN["mixed"], G_GEN["ffnb"] = 20, 21, 22
X_GEN["ret"], X_GEN["conv"], X_GEN["lru"], X_GEN["rms2"] = 12, 13, 14, 15

VEC = {}


def _vec_columns():
    at = 0
    for name, n in [("ln_g", 64), ("ln_b", 64), ("lb", 32), ("gnorm", 1), ("subln", 2), ("lam", 8), ("sinks", 16),
                    ("norm1", 8), ("mgb", 16), ("gnw", 8), ("lconvw", 32), ("lconvb", 8), ("br", 8), ("bi", 8),
                    ("lamb", 8), ("norm2", 8), ("fconvw", 72), ("fconvb", 24), ("normf", 8), ("invf", 1)]:
        VEC[name] = at
        at += n
    return at


NVEC = _vec_columns()

HG_LEVELS = [1, 2, 4, 8, 16, 32, 64]


class Own:

    def __init__(self, own):
        self.own, self.n, self.at, self.reg, self.per = own, {}, None, None, {}

    def sig(self, sem=None):
        sem = self.own if sem is None else sem
        self.n[sem.name] = self.n.get(sem.name, 0) + 1
        self.at = sem
        return sem, 1

    def others(self, sem, n):
        self.n[sem.name] = self.n.get(sem.name, 0) + n

    def value(self, sem):
        v = self.n.get(sem.name, 0)
        return v + self.reg * self.per.get(sem.name, 0) if self.reg is not None and self.per.get(sem.name, 0) else v

    def last(self):
        return self.at, self.value(self.at)

    def enter(self, reg, per):
        self.reg, self.per, self.n0, self.at = reg, {s.name: k for s, k in per.items()}, dict(self.n), None

    def leave(self, times):
        for name, k in self.n.items():
            d = k - self.n0.get(name, 0)
            assert d == self.per.get(name, 0), (name, d)
            self.n[name] = self.n0.get(name, 0) + d * times
        self.reg, self.per, self.at = None, {}, None


def build(nc, stream, xin, pin, pos, vecs, relb, onehot, eye, swap, picks, decay, resets, out):
    with ExitStack() as ctx:
        top = [16512]

        def place(name, shape, dt=F32, at=None):
            size = (int(np.prod(shape[1:])) * 4 + 31) // 32 * 32
            if at is None:
                at, top[0] = top[0], top[0] + size
            assert at + size <= nc.sbuf_usable_end, (name, at, size)
            return nc.alloc_sbuf_tensor_at(name, shape, dt, offset=at)

        raw = place("raw", [P, 2, 8, 256])
        whi = place("whi", [P, 2, 8, 256], F32R)
        wlo = place("wlo", [P, 2, 8, 256], F32R)
        h = place("h", [P, KT, S])
        xh = place("xh", [P, KT, S], F32R)
        xl = place("xl", [P, KT, S], F32R)
        gh = place("gh", [P, KT, S], F32R)
        gl = place("gl", [P, KT, S], F32R)
        vec = place("vec", [P, NVEC])
        ident = place("ident", [P, P])
        ones = place("ones", [P, P])
        swapm = place("swapm", [P, P])
        pick = place("pick", [P, len(HG_LEVELS), P], I32)
        one = place("one", [P, 8])
        reset = place("reset", [P, S])
        small = place("small", [P, 256])
        arena = (top[0] + 31) // 32 * 32

        class Arena:
            def __init__(self, at=0):
                self.at = arena + at

            def __call__(self, name, shape, dt=F32):
                t = place(name, shape, dt, at=self.at)
                self.at += (int(np.prod(shape[1:])) * 4 + 31) // 32 * 32
                return t

        a = Arena()
        s1 = a("s1", [P, 2, S])
        s2 = a("s2", [P, 2, S])
        sq = a("sq", [P, 2, 2, S])
        mean = a("mean", [P, S])
        rstd = a("rstd", [P, S])
        msq = a("msq", [P, S])
        tln = a("tln", [P, 2, S])
        ln_end = a.at - arena
        a = Arena(ln_end)
        rl = a("rl", [P, 2, S])
        hid = a("hid", [P, 2, S])
        po = a("po", [P, KT, S])
        pf = a("pf", [P, 2, S])
        ph = a("ph", [P, 2, S], F32R)
        plo = a("plo", [P, 2, S], F32R)
        sg = a("sg", [P, 2, 2, S])
        a = Arena()
        da_q = a("da_q", [P, 2, 2, S])
        da_k = a("da_k", [P, 2, 2, S])
        da_v = a("da_v", [P, 2, 4, 256])
        da_b = a("da_b", [P, 2, 2, S])
        da_s = a("da_s", [P, 2, 2, S])
        da_t = a("da_t", [P, 2, S])
        da_a = a("da_a", [P, 2, S])
        da_at = a("da_at", [P, 2, S])
        post_sq = a("post_sq", [P, S])
        post_rs = a("post_rs", [P, S])
        post_on = a("post_on", [P, S])
        a = Arena()
        hg_q = a("hg_q", [P, 2, 2, S])
        hg_k = a("hg_k", [P, 2, 2, S])
        hg_f = a("hg_f", [P, 2, 2, S])
        hg_v = a("hg_v", [P, 2, 4, 256])
        hg_g = a("hg_g", [P, 2, 2, S])
        hg_e = a("hg_e", [P, 2, S])
        hg_p = a("hg_p", [P, 2, S])
        hg_a = a("hg_a", [P, 4, P])
        hg_far = a("hg_far", [P, 6, P])
        hg_qd = a("hg_qd", [P, 4, P])
        hg_kd = a("hg_kd", [P, 4, P])
        hg_x = a("hg_x", [P, 4, P])
        hsq = a("hsq", [P, S])
        hrs = a("hrs", [P, S])
        hon = a("hon", [P, S])
        a = Arena()
        sw_k = a("sw_k", [P, 2, S])
        sw_v = a("sw_v", [P, 4, P])
        sw_q = a("sw_q", [P, 2, 2, S])
        sw_b = a("sw_b", [P, 2, 4, 256])
        sw_s = a("sw_s", [P, 2, 4, 256])
        sw_at = a("sw_at", [P, 2, 4, P])
        sw_o = a("sw_o", [P, 2, 2, P])
        a = Arena()
        rt_t = a("rt_t", [P, 2, S])
        rt_q = a("rt_q", [P, 2, S])
        rt_k = a("rt_k", [P, 2, S])
        rt_v = a("rt_v", [P, 2, 4, 256])
        rt_g_at = a.at - arena
        rt_g = a("rt_g", [P, 2, 2, S])
        rt_d = a("rt_d", [P, 4, S])
        rt_s = a("rt_s", [P, 2, S])
        rt_o = a("rt_o", [P, 2, S])
        rt_o2 = a("rt_o2", [P, 2, S])
        rt_m = a("rt_m", [P, S])
        rt_rs = a("rt_rs", [P, S])
        rt_end = a.at - arena
        rt_f = a("rt_f", [P, 2, S])
        cosf = a("cosf", [P, S])
        sinf = a("sinf", [P, S])
        sgt = Arena(rt_end)("sgt", [P, KT, S])
        a = Arena()
        mixt = a("mixt", [P, KT, S])
        xc = a("xc", [P, KT, S])
        lr = a("lr", [P, 2, S])
        la = a("la", [P, 2, S])
        lu = a("lu", [P, 2, S])
        li = a("li", [P, 2, S])
        a = Arena(ln_end)
        cv = a("cv", [P, 2, S])
        hid2 = a("hid2", [P, 2, S])
        fin = a("fin", [P, KT, S])
        a = Arena()
        tab = a("tab", [33, 1280])
        rb = a("rb", [33, 16])
        tabo = a("tabo", [16, 1280])
        a = Arena(rt_g_at)
        posi = a("posi", [P, S], I32)
        ang = a("ang", [P, S])
        turn = a("turn", [P, S])

        proj = ctx.enter_context(nc.psum_tensor("proj", [P, 4, S], F32))
        mix = ctx.enter_context(nc.psum_tensor("mix", [P, 4, S], F32))

        table = nc.dram_tensor("bias_table", [16, 1280], F32).ap()
        bias_da = nc.dram_tensor("bias_da", [16, P, S], F32).ap()
        bias_sw = nc.dram_tensor("bias_sw", [16, P, 256], F32).ap()

        def sem(name):
            return ctx.enter_context(nc.semaphore(name))

        raw_in = [sem("raw_in_even"), sem("raw_in_odd")]
        split_done = sem("split_done")
        pool_own = sem("pool_own")
        unit_done = sem("unit_done")
        rel = {"act": sem("banks_read_act"), "dve": sem("banks_read_dve")}
        xh_ready, xl_ready = sem("xh_ready"), sem("xl_ready")
        gh_ready, gl_ready = sem("gh_ready"), sem("gl_ready")
        act_own, dve_own = sem("act_own"), sem("dve_own")
        loaded = sem("loaded")
        x_in = [sem(f"x_in{t}") for t in range(4)]
        table_out, biased = sem("table_out"), sem("biased")
        m = {}

        def M(name):
            if name not in m:
                m[name] = sem(name)
            return m[name]

        for name in ("start_pe start_act start_dve relu_done s1_done sq_done s2_done stats mean_read msq_read "
                     "rstd_done ln_u ln_h ln_full low_even p_in p_hi p_lo h_new scores masked negmax expd coef second "
                     "attn transposed at_copied av o_sq o_ms o_std o_rstd o_norm z_done hg_ready hg_diff hg_exp "
                     "hg_prod hg_sc hg_pick hg_far_copied hg_fark hg_lf kdup kcopy rot_in rot_mm rot_done decay_in "
                     "rsc rmul rav ro_copied rst rn_done bias_in0 bias_in1 sw_bias0 sw_bias1 hi_even hg_ln hg_f "
                     "hg_fardiff hg_farexp hg_av sw_scores sw_masked sw_negmax sw_expd sw_attn sw_transposed "
                     "sw_at_copied sw_av sw_out sw_hi sw_lo pos_in trig z_ret r_mean rvar rstdd tap tap2 gelu2 stored "
                     "r_act u_act b_done hl_done z_lru mixed final_out lamsum lamexp lamprod").split():
            M(name)

        block = ctx.enter_context(nc.Block())

        def col(name, j=0, n=1):
            return vec[:, VEC[name] + j:VEC[name] + j + n]

        @block.sync
        def _(sp):
            for s in range(2):
                sp.dma_start(raw[:, s].rearrange("p k n -> p (k n)"), stream[s]).then_inc(raw_in[s], 16)
            with sp.Fori(1, N_SLABS // 2) as i:
                for s in range(2):
                    sp.wait_ge(split_done, i * 2 + (s - 1))
                    sp.dma_start(raw[:, s].rearrange("p k n -> p (k n)"),
                                 stream[bass.ds(i * 2 + s, 1), :, :].rearrange("a p n -> (a p) n")).then_inc(raw_in[s], 16)
            for n in range(N_SLABS // 2 * 2, N_SLABS):
                sp.wait_ge(split_done, n - 1)
                sp.dma_start(raw[:, n % 2].rearrange("p k n -> p (k n)"), stream[n]).then_inc(raw_in[n % 2], 16)
            for t in range(KT):
                sp.wait_ge(M("final_out"), t + 1)
                sp.dma_start(out[:, t, :], fin[:, t, :]).then_inc(M("stored"), 16)
            sp.wait_ge(M("stored"), KT * 16)

        @block.gpsimd
        def _(pool):
            def split(slot, raw_value, split_value, unit_value):
                pool.wait_ge(raw_in[slot], raw_value)
                if unit_value is not None:
                    pool.wait_ge(unit_done, unit_value)
                nc.gpsimd.tensor_tensor(whi[:, slot, 0], raw[:, slot, 0], one[:, 0:1].to_broadcast([P, 256]), ALU.mult).then_inc(pool_own, 1)
                nc.gpsimd.tensor_scalar(whi[:, slot, 1:], raw[:, slot, 1:], 1.0, 0.0, ALU.mult, ALU.add).then_inc(pool_own, 1)
                pool.wait_ge(pool_own, split_value * 2 + 1)
                nc.gpsimd.tensor_tensor(wlo[:, slot], raw[:, slot], whi[:, slot].bitcast(F32),
                                        ALU.subtract).then_inc(split_done, 1)

            def low_parts(l, gen):
                for k in range(KT):
                    pool.wait_ge(M("ln_full"), 8 * l + k + 1)
                    pool.wait_ge(*((xh_ready, 4 * gen + k // 2 + 1) if k % 2 else (M("ln_h"), 4 * l + k // 2 + 1)))
                    nc.gpsimd.tensor_tensor(xl[:, k, :], h[:, k, :], xh[:, k, :].bitcast(F32), ALU.subtract)\
                        .then_inc(xl_ready if k % 2 else M("low_even"), 1)

            norm_at = {}
            for layer in range(NL):
                norm_at[PLAN.at[f"ffn{layer}"][0] + 2] = (2 * layer, X_GEN[f"ln1{layer}"])
                norm_at[PLAN.at[f"gate{layer}"][0] + 2] = (2 * layer + 1, X_GEN[f"ln2{layer}"])

            nc.gpsimd.memset(one[:], 1.0).then_inc(pool_own, 1)
            pool.wait_ge(pool_own, 1)
            n = 0
            while n < N_SLABS:
                if n in norm_at:
                    low_parts(*norm_at[n])
                run = 0
                if n >= 3:
                    while n + run < N_SLABS and (run == 0 or n + run not in norm_at) and PLAN.last_unit[n + run - 2] - PLAN.last_unit[n - 2] == run:
                        run += 1
                if run >= 8:
                    pairs = run // 2
                    u0 = PLAN.last_unit[n - 2] + 1
                    with pool.Fori(0, pairs) as i:
                        for s in range(2):
                            slot = (n + s) % 2
                            split(slot, i * 16 + 16 * ((n + s) // 2 + 1), i * 2 + (n + s + 1), i * 2 + (u0 + s))
                    n += 2 * pairs
                else:
                    split(n % 2, 16 * (n // 2 + 1), n + 1, PLAN.last_unit[n - 2] + 1 if n >= 2 else None)
                    n += 1

        @block.tensor
        def _(pe):
            def passes(out, wparts, xparts, first, last, check=False):
                (wh, wl), (ah, al) = wparts, xparts
                nc.tensor.matmul(out, wh, ah, start=first, stop=False, skip_group_check=check)
                nc.tensor.matmul(out, wh, al, start=False, stop=False, skip_group_check=check)
                return nc.tensor.matmul(out, wl, ah, start=False, stop=last, skip_group_check=check)

            def begin_unit(u, slab_value=None, rel_wait="static"):
                pe.wait_ge(split_done, PLAN.unit_slab[u] + 1 if slab_value is None else slab_value)
                if rel_wait == "static":
                    if u >= 2:
                        e, v = PLAN.released(u - 2)
                        pe.wait_ge(rel[e], v)
                elif rel_wait is not None:
                    pe.wait_ge(*rel_wait)

            def feature_chunk(u, k, kn, w0, operand):
                slot = PLAN.unit_slab[u] % 2
                oh, ol = operand
                for j in range(2):
                    c = slice(j * P, (j + 1) * P)
                    last = passes(proj[:, 2 * (u % 2) + j, :], (whi[:, slot, w0 + k, c], wlo[:, slot, w0 + k, c]),
                                  (oh[:, k, :], ol[:, k, :]), k == 0, k == kn - 1)
                return last

            def token_chunk(u, k, kn, operand, c0=0, width=256, banks=(0, 1)):
                slot = PLAN.unit_slab[u] % 2
                oh, ol = operand
                per = 4 // len(banks)
                for st in range(4):
                    o = proj[:, 2 * (u % 2) + banks[st // per], (st % per) * width:(st % per + 1) * width]
                    t = slice(st * P, (st + 1) * P)
                    w = slice(c0, c0 + width)
                    ah, al, wh, wl = oh[:, k, t], ol[:, k, t], whi[:, slot, k, w], wlo[:, slot, k, w]
                    nc.tensor.matmul(o, ah, wh, start=k == 0 and st % per == 0, stop=False, skip_group_check=True)
                    nc.tensor.matmul(o, ah, wl, start=False, stop=False, skip_group_check=True)
                    last = nc.tensor.matmul(o, al, wh, start=False, stop=k == kn - 1, skip_group_check=True)
                return last

            def operand_wait(which, gen, k):
                if k % 2 == 0:
                    hi, lo = (xh_ready, xl_ready) if which == "x" else (gh_ready, gl_ready)
                    pe.wait_ge(hi, gen * 4 + k // 2 + 1)
                    pe.wait_ge(lo, gen * 4 + k // 2 + 1)

            X, G = (xh, xl), (gh, gl)

            def whole_unit(u, which, gen=None, token=False, kn=8, w0=0, operand=None, **begin):
                begin_unit(u, **begin)
                op = operand or (X if which == "x" else G)
                for k in range(kn):
                    if gen is not None:
                        operand_wait(which, gen, k)
                    last = token_chunk(u, k, kn, op) if token else feature_chunk(u, k, kn, w0, op)
                last.then_inc(unit_done, 1)

            def out_chunks(layer, first, end):
                u = PLAN.at[f"out{layer}"][1]
                for k in range(first, end):
                    if k == 0:
                        begin_unit(u)
                    operand_wait("x", X_GEN[f"mix{layer}"], k)
                    last = feature_chunk(u, k, 8, 0, X)
                    if k == 7:
                        last.then_inc(unit_done, 1)

            def stats(l, with_mean=True):
                if with_mean:
                    pe.wait_ge(M("s1_done"), l + 1)
                    nc.tensor.matmul(mix[:, 0, :], ones[:, :], s1[:, 0, :], start=True, stop=True).then_inc(M("stats"), 1)
                pe.wait_ge(M("s2_done"), 3 * (l + 1))
                nc.tensor.matmul(mix[:, 1, :], ones[:, :], s2[:, 0, :], start=True, stop=True).then_inc(M("stats"), 1)

            def start():
                pe.wait_ge(loaded, 16 * LOADS)
                pe.wait_ge(M("start_dve"), 1)
                for j in range(4):
                    last = nc.tensor.matmul(mix[0:16, j, 0:320], rb[:, :], tab[:, j * 320:(j + 1) * 320], start=True, stop=True)
                last.then_inc(M("start_pe"), 1)
                pe.wait_ge(M("lamprod"), 1)
                pe.wait_ge(M("start_act"), 1)
                nc.tensor.matmul(mix[:, 0, 0:4], ones[0:64, :], small[0:64, 0:4], start=True, stop=True).then_inc(M("lamsum"), 1)

            def da_mixer(d, layer):
                s0, u0 = PLAN.at[f"mix{layer}"]
                gen = G_GEN[f"in{layer}"]

                def chunk(g, c):
                    u = u0 + 3 * g + c // 8
                    k = c % 8
                    if k == 0:
                        begin_unit(u)
                    if g == 0 and c < 8:
                        operand_wait("g", gen, k)
                    last = token_chunk(u, k, 8, G) if c // 8 == 2 else feature_chunk(u, k, 8, 0, G)
                    if k == 7:
                        last.then_inc(unit_done, 1)

                def scores(k):
                    it = 32 * d + k
                    g, hh, qb = k // 8, k // 4 % 2, k % 4
                    if k % 8 == 0:
                        e, v = PLAN.released(u0 + 3 * g + 1)
                        pe.wait_ge(rel[e], v)
                    if it:
                        pe.wait_ge(M("masked"), 2 * it)
                    for mp in range(2):
                        r = slice(64 * mp, 64 * mp + 64)
                        last = nc.tensor.matmul(mix[:, mp, 0:(qb + 1) * P], da_q[r, g % 2, hh, qb * P:(qb + 1) * P],
                                                da_k[r, g % 2, hh, 0:(qb + 1) * P], start=True, stop=True)
                    last.then_inc(M("scores"), 1)

                def transposes(k):
                    it = 32 * d + k
                    qb = k % 4
                    pe.wait_ge(M("attn"), it + 1)
                    if it:
                        pe.wait_ge(M("at_copied"), it)
                    if k > 4 and k % 4 == 1:
                        pe.wait_ge(M("o_std"), post_base(layer) + k // 4)
                    for kb in range(qb + 1):
                        last = nc.tensor.transpose(mix[:, 2, kb * P:(kb + 1) * P], da_a[:, k % 2, kb * P:(kb + 1) * P], ident[:, :])
                    last.then_inc(M("transposed"), 1)

                def values(k):
                    it = 32 * d + k
                    g, hh, qb = k // 8, k // 4 % 2, k % 4
                    if k % 8 == 0:
                        e, v = PLAN.released(u0 + 3 * g + 2)
                        pe.wait_ge(rel[e], v)
                    pe.wait_ge(M("at_copied"), it + 1)
                    if qb == 0 and k:
                        pe.wait_ge(M("o_norm"), post_base(layer) + k // 4)
                    for kb in range(qb + 1):
                        last = nc.tensor.matmul(mix[:, 3, qb * P:(qb + 1) * P], da_v[:, g % 2, kb, hh * P:(hh + 1) * P],
                                                da_at[:, k % 2, kb * P:(kb + 1) * P], start=kb == 0, stop=kb == qb)
                    last.then_inc(M("av"), 1)

                def mean_square(k):
                    n = post_base(layer) + k // 4
                    pe.wait_ge(M("o_sq"), n + 1)
                    pe.wait_ge(M("at_copied"), 32 * d + min(k + 2, 32))
                    nc.tensor.matmul(mix[:, 2, :], ones[:, :], post_sq[:, :], start=True, stop=True).then_inc(M("o_ms"), 1)

                for c in range(24):
                    chunk(0, c)
                    if layer == 0 and c == 7:
                        start()
                if layer == 0:
                    pe.wait_ge(M("lamexp"), 1)
                for k in range(32 + 4):
                    if k < 32:
                        scores(k)
                    if k >= 7 and k % 4 == 3:
                        mean_square(k - 4)
                    if k < 24:
                        for c in range(3):
                            chunk(k // 8 + 1, 3 * (k % 8) + c)
                    elif k % 2 == 1:
                        out_chunks(layer, (k - 25) // 2, (k - 25) // 2 + 1)
                    if 2 <= k < 34:
                        transposes(k - 2)
                    if 3 <= k < 35:
                        values(k - 3)

            def hg_mixer(layer):
                s0, u0 = PLAN.at[f"mix{layer}"]
                gen = G_GEN[f"in{layer}"]

                def chunk(g, c):
                    u = u0 + 4 * g + c // 8
                    k = c % 8
                    if k == 0:
                        begin_unit(u)
                    if g == 0 and c < 8:
                        operand_wait("g", gen, k)
                    last = token_chunk(u, k, 8, G) if c // 8 == 2 else feature_chunk(u, k, 8, 0, G)
                    if k == 7:
                        last.then_inc(unit_done, 1)

                def level(hd, j):
                    g, hh = hd // 2, hd % 2
                    it = 8 * hd + j
                    bank = mix[:, it % 2, :]
                    if j == 0:
                        pe.wait_ge(M("hg_ready"), hd + 1)
                        e, v = PLAN.released(u0 + 4 * g + 1)
                        pe.wait_ge(rel[e], v)
                    else:
                        pe.wait_ge(M("hg_prod"), 7 * hd + j)
                    if it >= 2:
                        pe.wait_ge(M("hg_pick"), it - 1)
                    if j < 2 and hd:
                        pe.wait_ge(M("hg_far_copied"), 2 * hd)
                    for t in range(4):
                        c = slice(t * P, (t + 1) * P)
                        if j == 0:
                            last = nc.tensor.matmul(bank[:, c], hg_k[:, g % 2, hh, c], hg_q[:, g % 2, hh, c], start=True, stop=True)
                        else:
                            b = (7 * hd + j - 1) % 2
                            last = nc.tensor.matmul(bank[:, c], hg_p[:, b, c], hg_p[:, b, c], start=True, stop=True)
                    last.then_inc(M("hg_sc"), 1)

                def far(hd):
                    pe.wait_ge(M("hg_fark"), hd + 1)
                    pe.wait_ge(M("hg_pick"), 8 * hd + 8)
                    nc.tensor.matmul(mix[:, 0, 0:P], hg_kd[:, 0, :], hg_qd[:, 0, :], start=True, stop=True)
                    nc.tensor.matmul(mix[:, 0, P:3 * P], hg_kd[:, 3, :], hg_qd[:, 1:3, :], start=True, stop=True)
                    nc.tensor.matmul(mix[:, 1, 0:2 * P], hg_kd[:, 1, :], hg_qd[:, 1:3, :], start=True, stop=True)
                    nc.tensor.matmul(mix[:, 1, 2 * P:3 * P], hg_kd[:, 2, :], hg_qd[:, 3, :], start=True, stop=True)\
                        .then_inc(M("hg_sc"), 1)

                def values(hd):
                    g, hh = hd // 2, hd % 2
                    pe.wait_ge(M("hg_far_copied"), 2 * (hd + 1))
                    e, v = PLAN.released(u0 + 4 * g + 2)
                    pe.wait_ge(rel[e], v)
                    n = post_base(layer) + hd
                    if hd:
                        pe.wait_ge(M("o_norm"), n)
                    v_ = lambda t: hg_v[:, g % 2, t, hh * P:(hh + 1) * P]
                    where = {(0, 1): 0, (0, 2): 1, (0, 3): 2, (1, 2): 3, (1, 3): 4, (2, 3): 5}
                    for t in range(4):
                        for s in range(t + 1):
                            src = hg_a[:, t, :] if s == t else hg_far[:, where[s, t], :]
                            last = nc.tensor.matmul(mix[:, 3, t * P:(t + 1) * P], v_(s), src, start=s == 0, stop=s == t)
                    last.then_inc(M("hg_av"), 1)
                    pe.wait_ge(M("o_sq"), n + 1)
                    if hd:
                        pe.wait_ge(M("o_std"), n)
                    nc.tensor.matmul(mix[:, 2, :], ones[:, :], hsq[:, :], start=True, stop=True).then_inc(M("o_ms"), 1)

                for c in range(32):
                    chunk(0, c)
                for k in range(8 * 10):
                    hd, j = k // 10, k % 10
                    if k < 60:
                        g1, kk = k // 20 + 1, k % 20
                        for c in range(kk * 32 // 20, (kk + 1) * 32 // 20):
                            chunk(g1, c)
                    if j < 8:
                        level(hd, j)
                    elif j == 8:
                        far(hd)
                    else:
                        values(hd)
                    if k >= 60:
                        out_chunks(layer, (k - 60) * 6 // 20, (k - 59) * 6 // 20)

            def sw_mixer(layer):
                s0, u0 = PLAN.at[f"mix{layer}"]
                gen = G_GEN[f"in{layer}"]
                begin_unit(u0)
                for k in range(8):
                    operand_wait("g", gen, k)
                    slot = PLAN.unit_slab[u0] % 2
                    passes(proj[:, 2 * (u0 % 2), :], (whi[:, slot, k, 0:P], wlo[:, slot, k, 0:P]), (gh[:, k, :], gl[:, k, :]), k == 0, k == 7)
                    last = token_chunk(u0, k, 8, G, c0=P, width=P, banks=(1,))
                last.then_inc(unit_done, 1)

                def chunk(g, c):
                    u = u0 + 1 + g
                    if c == 0:
                        begin_unit(u)
                    last = feature_chunk(u, c, 8, 0, G)
                    if c == 7:
                        last.then_inc(unit_done, 1)

                def scores(k):
                    g, n = k // 4, k % 4
                    if n == 0:
                        e, v = PLAN.released(u0 + 1 + g)
                        pe.wait_ge(rel[e], v)
                    if k == 0:
                        pe.wait_ge(M("kdup"), 32)
                    else:
                        pe.wait_ge(M("sw_masked"), 4 * k)
                    k0 = max(n - 1, 0) * P
                    kn = (n + 1) * P - k0
                    for hd in (0, 2, 1, 3):
                        r = slice(64 * (hd % 2), 64 * (hd % 2) + 64)
                        last = nc.tensor.matmul(mix[:, hd % 2, (hd // 2) * 256:(hd // 2) * 256 + kn],
                                                sw_q[r, g % 2, hd // 2, n * P:(n + 1) * P], sw_k[r, g // 2, k0:k0 + kn],
                                                start=True, stop=True)
                    last.then_inc(M("sw_scores"), 1)

                def transposes(k, kb):
                    q = sw_q_index(k, kb)
                    pe.wait_ge(M("sw_attn"), k + 1)
                    if q:
                        pe.wait_ge(M("sw_at_copied"), q)
                    for i, hd in enumerate((0, 2, 1, 3)):
                        last = nc.tensor.transpose(mix[:, 2, i * P:(i + 1) * P], sw_s[:, k % 2, hd, kb * P:(kb + 1) * P], ident[:, :])
                    last.then_inc(M("sw_transposed"), 1)

                def values(k, kb):
                    g, n = k // 4, k % 4
                    q = sw_q_index(k, kb)
                    pe.wait_ge(M("sw_at_copied"), q + 1)
                    if kb == 0 and k:
                        pe.wait_ge(M("sw_out"), k)
                    key = max(n - 1, 0) + kb
                    for par in range(2):
                        last = nc.tensor.matmul(mix[64 * par:64 * par + 64, 3, 0:256], sw_v[:, key, (g // 2) * 64:(g // 2) * 64 + 64],
                                                sw_at[:, q % 2, 2 * par:2 * par + 2, :], start=kb == 0, stop=kb == sw_blocks(n) - 1)
                    last.then_inc(M("sw_av"), 1)

                for c in range(8):
                    chunk(0, c)
                before = None
                for k in range(16 + 3):
                    if k < 12:
                        for c in range(2):
                            chunk(k // 4 + 1, 2 * (k % 4) + c)
                    if k < 16:
                        scores(k)
                    if 2 <= k < 18:
                        for kb in range(sw_blocks((k - 2) % 4)):
                            transposes(k - 2, kb)
                            if before:
                                values(*before)
                            before = (k - 2, kb)
                    if 13 <= k:
                        out_chunks(layer, k - 13, k - 12)
                values(*before)

            def ffn(layer):
                s0, u0 = PLAN.at[f"ffn{layer}"]
                base = PLAN.released(u0 + 0)[1] - 1
                xg, gg = X_GEN[f"ln1{layer}"], G_GEN[f"ffn{layer}"]
                for w in (u0 - 2, u0 - 1):
                    e, v = PLAN.released(w)
                    pe.wait_ge(rel[e], v)
                with pe.Fori(0, 4) as q:
                    for j in range(8):
                        u = u0 + j
                        begin_unit(u, slab_value=q * 8 + (s0 + j + 1), rel_wait=(rel["dve"], q * 8 + (base + j - 1)))
                        for k in range(8):
                            if j < 4:
                                operand_wait("x", xg, k)
                                last = feature_chunk(u, k, 8, 0, X)
                            else:
                                if k % 2 == 0:
                                    pe.wait_ge(gh_ready, q * 4 + (gg * 4 + k // 2 + 1))
                                    pe.wait_ge(gl_ready, q * 4 + (gg * 4 + k // 2 + 1))
                                last = feature_chunk(u, k, 8, 0, G)
                        last.then_inc(unit_done, 1)

            for layer in range(NL):
                if layer % 3 == 0:
                    da_mixer(layer // 3, layer)
                elif layer == 1:
                    hg_mixer(layer)
                else:
                    sw_mixer(layer)
                s0, u0 = PLAN.at[f"out{layer}"]
                out_chunks(layer, 6, 8)
                for j in range(1, 4):
                    whole_unit(u0 + j, "x", X_GEN[f"mix{layer}"])
                stats(2 * layer)
                ffn(layer)
                s0, u0 = PLAN.at[f"ple{layer}"]
                pe.wait_ge(M("p_hi"), layer + 1)
                pe.wait_ge(M("p_lo"), layer + 1)
                for j in range(4):
                    whole_unit(u0 + j, "p", kn=2, w0=2 * j, operand=(ph, plo))
                    if j == 1:
                        stats(2 * layer + 1)
                s0, u0 = PLAN.at[f"gate{layer}"]
                for j in range(4):
                    whole_unit(u0 + j, "x", X_GEN[f"ln2{layer}"])

            stats(8, with_mean=False)

            def ret_mixer():
                s0, u0 = PLAN.at["ret"]
                gen = G_GEN["in4"]
                def chunks(u, first, end):
                    for c in range(first, end):
                        v, k = u + c // 8, c % 8
                        if k == 0:
                            begin_unit(v)
                        if v == u0:
                            operand_wait("g", gen, k)
                        last = token_chunk(v, k, 8, G) if v - u0 in (2, 3, 8, 9) else feature_chunk(v, k, 8, 0, G)
                        if k == 7:
                            last.then_inc(unit_done, 1)

                def rotate(g, j):
                    n = 2 * g + j
                    e, v = PLAN.released(u0 + 6 * g + j)
                    pe.wait_ge(rel[e], v)
                    if n:
                        pe.wait_ge(M("rot_done"), 2 * n)
                    for hh in range(2):
                        last = nc.tensor.matmul(mix[:, hh, :], swapm[:, :], rt_f[:, hh, :], start=True, stop=True)
                    last.then_inc(M("rot_mm"), 1)

                for g in range(2):
                    u = u0 + 6 * g
                    chunks(u, 0, 10)
                    rotate(g, 0)
                    chunks(u, 10, 18)
                    rotate(g, 1)
                    chunks(u, 18, 32)
                    fill, share = 32, (1, 1, 1, 1, 2, 2) if g == 0 else (2, 2, 2, 2, 4, 4)
                    for hh in range(2):
                        hd = 2 * g + hh
                        pe.wait_ge(M("rot_done"), 2 * (2 * g + 2))
                        for kb in range(4):
                            n = 4 * hd + kb
                            w = S - kb * P
                            if n >= 2:
                                pe.wait_ge(M("rmul"), n - 1)
                            nc.tensor.matmul(mix[:, n % 2, 0:w], rt_k[:, hh, kb * P:(kb + 1) * P], rt_q[:, hh, kb * P:S],
                                             start=True, stop=True).then_inc(M("rsc"), 1)
                            chunks(u, fill, fill + share[kb])
                            fill += share[kb]
                            if kb == 0:
                                e, v = PLAN.released(u0 + 6 * g + 3)
                                pe.wait_ge(rel[e], v)
                                if hd:
                                    pe.wait_ge(M("ro_copied"), 2 * hd)
                            pe.wait_ge(M("rmul"), n + 1)
                            for t in range(2):
                                last = nc.tensor.matmul(mix[:, 2 + t, kb * P:S], rt_v[:, hh, kb, t * P:(t + 1) * P],
                                                        rt_s[:, n % 2, 0:w], start=kb == 0, stop=kb == 3)
                            last.then_inc(M("rav"), 1)
                        chunks(u, fill, fill + share[4])
                        fill += share[4]
                        pe.wait_ge(M("ro_copied"), 2 * hd + 2)
                        for src, b in ((rt_o, 0), (rt_o2, 1)):
                            for t in range(2):
                                last = nc.tensor.matmul(mix[:, b, :], ones[:, :], src[:, t, :], start=t == 0, stop=t == 1)
                        last.then_inc(M("rst"), 1)
                        chunks(u, fill, fill + share[5])
                        fill += share[5]
                        pe.wait_ge(M("rn_done"), hd + 1)
                        pe.wait_ge(M("r_mean"), 2 * (hd + 1))

            ret_mixer()
            for name, which, gen in (("gret", "g", None), ("reto", "x", X_GEN["ret"]), ("xlru", "g", None)):
                s0, u0 = PLAN.at[name]
                for j in range(2 if name == "gret" else 0, 4):
                    whole_unit(u0 + j, which, gen)
            s0, u0 = PLAN.at["lru"]
            for n in range(4):
                whole_unit(u0 + 3 * n, "g")
                for t in range(2):
                    u = u0 + 3 * n + 1 + t
                    begin_unit(u)
                    operand_wait("x", X_GEN["conv"], 2 * n)
                    for k in range(2):
                        last = feature_chunk(u, k, 2, 4 * (n % 2) + 2 * t, (xh[:, 2 * n:2 * n + 2, :], xl[:, 2 * n:2 * n + 2, :]))
                    last.then_inc(unit_done, 1)
            for name, which, gen in (("ylru", "g", None), ("lruo", "x", X_GEN["lru"]),
                                     ("wout", "g", G_GEN["mixed"])):
                s0, u0 = PLAN.at[name]
                for j in range(4):
                    whole_unit(u0 + j, which, gen)
            stats(9, with_mean=False)
            s0, u0 = PLAN.at["ffnb"]
            base = PLAN.released(u0)[1] - 1
            for w in (u0 - 2, u0 - 1):
                e, v = PLAN.released(w)
                pe.wait_ge(rel[e], v)
            with pe.Fori(0, 3) as q:
                for j in range(12):
                    u = u0 + j
                    begin_unit(u, slab_value=q * 12 + (s0 + j + 1), rel_wait=(rel["dve"], q * 12 + (base + j - 1)))
                    for k in range(8):
                        if j < 8:
                            operand_wait("x", X_GEN["rms2"], k)
                            last = feature_chunk(u, k, 8, 0, X)
                        else:
                            if k % 2 == 0:
                                pe.wait_ge(gh_ready, q * 4 + (G_GEN["ffnb"] * 4 + k // 2 + 1))
                                pe.wait_ge(gl_ready, q * 4 + (G_GEN["ffnb"] * 4 + k // 2 + 1))
                            last = feature_chunk(u, k, 8, 0, G)
                    last.then_inc(unit_done, 1)
            stats(10, with_mean=False)

        @block.scalar
        def _(act):
            own = Own(act_own)
            A = nc.scalar.activation

            def mine():
                act.wait_ge(*own.last())

            def banks(u):
                return proj[:, 2 * (u % 2):2 * (u % 2) + 2, :]

            def done(u):
                act.wait_ge(unit_done, u + 1)

            for t in range(4):
                p2 = slice(2 * t, 2 * t + 2)
                act.dma_start(h[:, p2, :], xin[:, p2, :]).then_inc(x_in[t], 16)
            for dst, src in ((vec[:, :], vecs), (ident[:, :], eye), (swapm[:, :], swap), (pick[:, :, :], picks),
                             (reset[:, :], resets), (tab[:, :], onehot), (rb[0:32, :], relb)):
                act.dma_start(dst, src).then_inc(loaded, 16)
            for t in range(4):
                p2 = slice(2 * t, 2 * t + 2)
                act.wait_ge(x_in[t], 16)
                A(gh[:, p2, :], h[:, p2, :], ACT.Copy).then_inc(*own.sig(gh_ready))
            act.wait_ge(M("start_pe"), 1)
            A(tabo[:, :].rearrange("p (a b) -> p a b", a=4), mix[0:16, :, 0:320], ACT.Copy).then_inc(*own.sig(M("start_act")))
            mine()
            act.dma_start(table, tabo[:, :]).then_inc(table_out, 16)
            act.wait_ge(table_out, 16)
            act.dma_start(bias_da, bass.AP(tensor=table.tensor, offset=127, ap=[[1280, 16], [-1, P], [1, S]])).then_inc(biased, 16)
            act.dma_start(bias_sw, bass.AP(tensor=table.tensor, offset=640 + 383, ap=[[1280, 16], [-1, P], [1, 256]])).then_inc(biased, 16)
            act.wait_ge(M("lamsum"), 1)
            A(small[:, 4:8], mix[:, 0, 0:4], ACT.Exp).then_inc(*own.sig(M("lamexp")))
            act.wait_ge(M("start_dve"), 2)
            A(small[:, 64:96], small[:, 64:96], ACT.Exp).then_inc(*own.sig(M("lamexp")))
            A(small[:, 44:52], col("lamb", 0, 8), ACT.Abs).then_inc(*own.sig())
            mine()
            A(small[:, 44:52], small[:, 44:52], ACT.Exp, scale=-1.0).then_inc(*own.sig(M("lamexp")))

            def ln_squares(u, j, l):
                act.wait_ge(rel["dve"], PLAN.released(u)[1])
                if j >= 2:
                    act.wait_ge(M("s2_done"), 3 * l + j - 1)
                A(sq[:, j % 2], h[:, 2 * j:2 * j + 2, :], ACT.Square).then_inc(*own.sig(M("sq_done")))

            def warm(func):
                A(small[:, 253:254], small[:, 252:253], func).then_inc(*own.sig())

            def ln_apply(l, i, which):
                act.wait_ge(M("stats"), 2 * l + 1)
                A(mean[:, :], mix[:, 0, :], ACT.Copy, scale=1.0 / D).then_inc(*own.sig(M("mean_read")))
                mine()
                A(msq[:, :], mean[:, :], ACT.Square).then_inc(*own.sig(M("mean_read")))
                mine()
                warm(ACT.Sqrt)
                act.wait_ge(M("msq_read"), 2 * (l + 1))
                A(rstd[:, :], rstd[:, :], ACT.Sqrt).then_inc(*own.sig(M("rstd_done")))
                c = (2 * i + which) * 8
                for k in range(8):
                    act.wait_ge(M("ln_u"), 8 * l + k + 1)
                    A(xh[:, k, :], tln[:, k % 2, :], ACT.Identity, scale=col("ln_g", c + k), bias=col("ln_b", c + k))\
                        .then_inc(*own.sig(xh_ready if k % 2 else M("ln_h")))

            def rms_apply(l, name, out_hi, hi_sem):
                mine()
                warm(ACT.Sqrt)
                act.wait_ge(M("msq_read"), 2 * (l + 1))
                A(rstd[:, :], rstd[:, :], ACT.Sqrt).then_inc(*own.sig(M("rstd_done")))
                for k in range(8):
                    act.wait_ge(M("ln_u"), 8 * l + k + 1)
                    if out_hi is None:
                        A(fin[:, k, :], tln[:, k % 2, :], ACT.Copy, scale=col(name, k)).then_inc(*own.sig(M("final_out")))
                    else:
                        A(out_hi[:, k, :], tln[:, k % 2, :], ACT.Copy, scale=col(name, k)).then_inc(*own.sig(hi_sem if k % 2 else M("ln_h")))

            def head_square(n, av_sem, av_value, buf):
                act.wait_ge(av_sem, av_value)
                if n:
                    act.wait_ge(M("o_ms"), n)
                A(buf[:, :], mix[:, 3, :], ACT.Square).then_inc(*own.sig(M("o_sq")))

            def head_std(n, buf):
                act.wait_ge(M("o_ms"), n + 1)
                if n:
                    act.wait_ge(M("o_norm"), n)
                mine()
                A(buf[:, :], mix[:, 2, :], ACT.Ln, scale=1.0 / P, bias=small[:, 252:253]).then_inc(*own.sig(M("o_std")))
                mine()
                A(buf[:, :], buf[:, :], ACT.Exp, scale=-0.5).then_inc(*own.sig(M("o_rstd")))

            def da_mixer(d, layer):
                s0, u0 = PLAN.at[f"mix{layer}"]

                def bias_in(hd):
                    if hd >= 2:
                        act.wait_ge(M("masked"), 64 * d + 8 * (hd - 1))
                    act.dma_start(da_b[:, hd % 2], bias_da[2 * hd:2 * hd + 2].rearrange("m p j -> p m j"))\
                        .then_inc(M(f"bias_in{hd % 2}"), 16)

                def evac(g, j):
                    u = u0 + 3 * g + j
                    done(u)
                    if g >= 2:
                        act.wait_ge(M("av"), 32 * d + 8 * (g - 1))
                        act.wait_ge(M("scores"), 32 * d + 8 * (g - 1))
                    if j == 0:
                        ins = A(da_q[:, g % 2], banks(u), ACT.Copy, scale=0.125)
                    elif j == 1:
                        ins = A(da_k[:, g % 2], banks(u), ACT.Copy)
                    else:
                        ins = A(da_v[:, g % 2].rearrange("p (b s) n -> p b (s n)", b=2), banks(u), ACT.Copy)
                    ins.then_inc(*own.sig(rel["act"]))

                def exps(k):
                    it, qb = 32 * d + k, k % 4
                    w = (qb + 1) * P
                    act.wait_ge(M("negmax"), it + 1)
                    for mp in range(2):
                        A(da_s[:, k % 2, mp, 0:w], da_s[:, k % 2, mp, 0:w], ACT.Exp, bias=small[:, 104 + 2 * (k % 2) + mp:105 + 2 * (k % 2) + mp],
                          accum_out=small[:, 108 + 2 * (k % 2) + mp:109 + 2 * (k % 2) + mp]).then_inc(*own.sig(M("expd")))

                def second(k):
                    it, qb = 32 * d + k, k % 4
                    w = (qb + 1) * P
                    act.wait_ge(M("coef"), it + 1)
                    if it >= 2:
                        act.wait_ge(M("attn"), it - 1)
                    mine()
                    A(da_t[:, k % 2, 0:w], da_s[:, k % 2, 1, 0:w], ACT.Copy, scale=small[:, 114 + 2 * (k % 2):115 + 2 * (k % 2)])\
                        .then_inc(*own.sig(M("second")))

                def at_copy(k):
                    it, qb = 32 * d + k, k % 4
                    act.wait_ge(M("transposed"), it + 1)
                    if it >= 2:
                        act.wait_ge(M("av"), it - 1)
                    A(da_at[:, k % 2, 0:(qb + 1) * P], mix[:, 2, 0:(qb + 1) * P], ACT.Copy).then_inc(*own.sig(M("at_copied")))

                def head_hi(hd):
                    n = post_base(layer) + hd
                    act.wait_ge(M("o_norm"), n + 1)
                    A(xh[:, hd, :], post_on[:, :], ACT.Copy, scale=small[:, 10 + d:11 + d]).then_inc(*own.sig(xh_ready if hd % 2 else M("hi_even")))

                evac(0, 0)
                evac(0, 1)
                act.wait_ge(biased, 32)
                bias_in(0)
                bias_in(1)
                evac(0, 2)
                for k in range(32 + 5):
                    if k < 33 and k % 8 == 0 and 1 <= k // 8 < 4:
                        evac(k // 8, 2)
                    if 1 <= k < 33:
                        second(k - 1)
                    if k < 32:
                        exps(k)
                        if k % 4 == 3 and k // 4 + 2 < 8:
                            bias_in(k // 4 + 2)
                    if k < 24 and k % 8 == 3:
                        evac(k // 8 + 1, 0)
                    if k < 24 and k % 8 == 6:
                        evac(k // 8 + 1, 1)
                    if k >= 7 and k % 4 == 3:
                        head_hi((k - 7) // 4)
                    if 2 <= k < 34:
                        at_copy(k - 2)
                    if 3 <= k < 35 and (k - 3) % 4 == 3:
                        n = post_base(layer) + (k - 3) // 4
                        head_square(n, M("av"), 32 * d + k - 3 + 1, post_sq)
                        head_std(n, post_rs)

            def hg_mixer(layer):
                s0, u0 = PLAN.at[f"mix{layer}"]

                def evac(g, j):
                    u = u0 + 4 * g + j
                    done(u)
                    dst = (hg_f, hg_q, hg_v, hg_g)[j]
                    if g >= 2:
                        act.wait_ge(M("hg_av"), 2 * (g - 1))
                        act.wait_ge(M("z_done"), 2 * (g - 1))
                    if j == 2:
                        ins = A(dst[:, g % 2].rearrange("p (b s) n -> p b (s n)", b=2), banks(u), ACT.Copy)
                    else:
                        ins = A(dst[:, g % 2], banks(u), ACT.Sigmoid if j == 0 else ACT.Silu)
                    ins.then_inc(*own.sig(rel["act"]))

                def logs(g):
                    act.wait_ge(M("hg_lf"), 2 * (g + 1))
                    A(hg_f[:, g % 2], hg_f[:, g % 2], ACT.Ln).then_inc(*own.sig(M("hg_ln")))

                def exp(hd, j):
                    n = 7 * hd + j - 1
                    act.wait_ge(M("hg_diff"), n + 1)
                    A(hg_e[:, n % 2, :], hg_e[:, n % 2, :], ACT.Exp).then_inc(*own.sig(M("hg_exp")))

                def far_exps(hd):
                    act.wait_ge(M("hg_fardiff"), hd + 1)
                    if hd:
                        act.wait_ge(M("hg_fark"), hd)
                    A(hg_x[:, :, :], hg_f[:, hd // 2 % 2, hd % 2, :].rearrange("p (t c) -> p t c", t=4), ACT.Exp).then_inc(*own.sig())
                    A(hg_kd[:, 0:4, :], hg_kd[:, 0:4, :], ACT.Exp).then_inc(*own.sig(M("hg_farexp")))

                def far_copy(hd):
                    act.wait_ge(M("hg_sc"), 9 * (hd + 1))
                    if hd:
                        act.wait_ge(M("hg_av"), hd)
                    for b in range(2):
                        A(hg_far[:, 3 * b:3 * b + 3, :], mix[:, b, 0:3 * P].rearrange("p (a b) -> p a b", a=3), ACT.Copy)\
                            .then_inc(*own.sig(M("hg_far_copied")))

                def head_hi(hd):
                    act.wait_ge(M("z_done"), hd + 1)
                    A(xh[:, hd, :], hon[:, :], ACT.Copy).then_inc(*own.sig(xh_ready if hd % 2 else M("hi_even")))

                for j in range(4):
                    evac(0, j)
                    if j == 1:
                        logs(0)
                for k in range(81):
                    hd, j = k // 10, k % 10
                    g, kk = k // 20, k % 20
                    if kk == 0 and 1 <= g < 4:
                        evac(g, 3)
                    if k < 60 and kk in (5, 10, 15):
                        evac(g + 1, kk // 5 - 1)
                    if k < 60 and kk == 7:
                        logs(g + 1)
                    if k < 80 and j < 7:
                        exp(hd, j + 1)
                    if k < 80 and j == 6:
                        far_exps(hd)
                    if j == 2 and hd:
                        head_hi(hd - 1)
                    if j == 8:
                        far_copy(hd)
                    if j == 9:
                        n = post_base(layer) + hd
                        head_square(n, M("hg_av"), hd + 1, hsq)
                        head_std(n, hrs)
                head_hi(7)

            def sw_mixer(layer):
                s0, u0 = PLAN.at[f"mix{layer}"]
                xg = X_GEN[f"mix{layer}"]

                def bias_in(g):
                    if g >= 2:
                        act.wait_ge(M("sw_masked"), 16 * (g - 1))
                    act.dma_start(sw_b[:, g % 2], bias_sw[4 * g:4 * g + 4].rearrange("m p j -> p m j")).then_inc(M(f"sw_bias{g % 2}"), 16)

                def evac(g):
                    done(u0 + 1 + g)
                    if g >= 2:
                        act.wait_ge(M("sw_scores"), 4 * (g - 1))
                    A(sw_q[:, g % 2], banks(u0 + 1 + g), ACT.Copy, scale=0.125).then_inc(*own.sig(rel["act"]))

                def exps(k):
                    kn = sw_blocks(k % 4) * P
                    act.wait_ge(M("sw_negmax"), k + 1)
                    b = k % 2
                    for hd in range(4):
                        A(sw_s[:, b, hd, 0:kn], sw_s[:, b, hd, 0:kn], ACT.Exp, bias=small[:, 124 + 4 * b + hd:125 + 4 * b + hd],
                          accum_out=small[:, 132 + 4 * b + hd:133 + 4 * b + hd]).then_inc(*own.sig())
                    A(small[:, 140 + 4 * b:144 + 4 * b], small[:, 140 + 4 * b:144 + 4 * b], ACT.Exp).then_inc(*own.sig(M("sw_expd")))

                def at_copy(q):
                    act.wait_ge(M("sw_transposed"), q + 1)
                    if q >= 2:
                        act.wait_ge(M("sw_av"), q - 1)
                    A(sw_at[:, q % 2], mix[:, 2, :].rearrange("p (a b) -> p a b", a=4), ACT.Copy).then_inc(*own.sig(M("sw_at_copied")))

                def hi(k):
                    g, n = k // 4, k % 4
                    act.wait_ge(M("sw_av"), sw_q_index(k, sw_blocks(n) - 1) + 1)
                    if k >= 2:
                        g2, n2 = (k - 2) // 4, (k - 2) % 4
                        act.wait_ge(*((xl_ready, 4 * xg + g2 + 1) if n2 == 3 else (M("sw_lo"), 3 * g2 + n2 + 1)))
                    A(sw_o[:, k % 2], mix[:, 3, 0:256].rearrange("p (a b) -> p a b", a=2), ACT.Copy).then_inc(*own.sig(M("sw_out")))
                    mine()
                    A(xh[:, 2 * g:2 * g + 2, n * P:(n + 1) * P], sw_o[:, k % 2], ACT.Copy)\
                        .then_inc(*own.sig(xh_ready if n == 3 else M("sw_hi")))

                bias_in(0)
                bias_in(1)
                done(u0)
                kb = proj[:, 2 * (u0 % 2), :]
                for c in range(2):
                    r = slice(64 * c, 64 * c + 64)
                    A(sw_k[r, c, :], kb[r, :], ACT.Copy).then_inc(*own.sig(M("kcopy")))
                A(sw_v[:, :, :].rearrange("p s n -> p (s n)"), proj[:, 2 * (u0 % 2) + 1, :], ACT.Copy).then_inc(*own.sig(rel["act"]))
                act.wait_ge(M("kcopy"), 2)
                act.dma_start(sw_k[64:128, 0, :], sw_k[0:64, 0, :]).then_inc(M("kdup"), 16)
                act.dma_start(sw_k[0:64, 1, :], sw_k[64:128, 1, :]).then_inc(M("kdup"), 16)
                evac(0)
                for k in range(16 + 4):
                    if k < 16 and k % 4 == 0 and k:
                        evac(k // 4)
                    if 2 <= k < 18:
                        for b in range(sw_blocks((k - 2) % 4)):
                            at_copy(sw_q_index(k - 2, b))
                    if 3 <= k < 19:
                        hi(k - 3)
                    if k < 16:
                        exps(k)
                        if k % 4 == 3 and k // 4 + 2 < 4:
                            bias_in(k // 4 + 2)

            def ffn(layer):
                s0, u0 = PLAN.at[f"ffn{layer}"]
                base = PLAN.released(u0)[1] - 1
                per = {M("relu_done"): 4, gh_ready: 4}

                def quarter(q):
                    for j in range(4):
                        act.wait_ge(unit_done, q * 8 + (u0 + j + 1) if q is not None else u0 + j + 25)
                        A(rl[:, :, :], banks(u0 + j), ACT.Relu).then_inc(*own.sig(M("relu_done")))
                        act.wait_ge(rel["dve"], q * 8 + (base + j + 1) if q is not None else base + j + 25)
                        A(gh[:, 2 * j:2 * j + 2, :], hid[:, :, :], ACT.Copy).then_inc(*own.sig(gh_ready))

                with act.Fori(0, 3) as q:
                    own.enter(q, per)
                    quarter(q)
                    own.leave(3)
                quarter(None)

            for layer in range(NL):
                if layer % 3 == 0:
                    da_mixer(layer // 3, layer)
                elif layer == 1:
                    hg_mixer(layer)
                else:
                    sw_mixer(layer)
                s0, u0 = PLAN.at[f"out{layer}"]
                for j in range(4):
                    ln_squares(u0 + j, j, 2 * layer)
                ln_apply(2 * layer, layer, 0)
                act.wait_ge(xl_ready, 4 * (X_GEN[f"ln1{layer}"] + 1))
                act.dma_start(pf[:, :, :], pin[layer]).then_inc(M("p_in"), 16)
                act.wait_ge(M("p_in"), 16 * (layer + 1))
                A(ph[:, :, :], pf[:, :, :], ACT.Copy).then_inc(*own.sig(M("p_hi")))
                ffn(layer)
                s0, u0 = PLAN.at[f"ffn{layer}"]
                for j in range(4):
                    ln_squares(u0 + 28 + j, j, 2 * layer + 1)
                s0, u0 = PLAN.at[f"ple{layer}"]
                for j in range(4):
                    done(u0 + j)
                    A(po[:, 2 * j:2 * j + 2, :], banks(u0 + j), ACT.Copy).then_inc(*own.sig(rel["act"]))
                ln_apply(2 * layer + 1, layer, 1)
                s0, u0 = PLAN.at[f"gate{layer}"]
                for j in range(4):
                    done(u0 + j)
                    if layer * 4 + j >= 2:
                        act.wait_ge(M("h_new"), layer * 4 + j - 1)
                    A(sg[:, j % 2], banks(u0 + j), ACT.Sigmoid).then_inc(*own.sig(rel["act"]))
                    p2 = slice(2 * j, 2 * j + 2)
                    act.wait_ge(M("h_new"), layer * 4 + j + 1)
                    if layer < NL - 1:
                        A(gh[:, p2, :], h[:, p2, :], ACT.Copy).then_inc(*own.sig(gh_ready))
                    else:
                        if j >= 2:
                            act.wait_ge(M("s2_done"), 3 * 8 + j - 1)
                        A(sq[:, j % 2], h[:, p2, :], ACT.Square).then_inc(*own.sig(M("sq_done")))

            rms_apply(8, "norm1", gh, gh_ready)
            s0, u0 = PLAN.at["ret"]
            act.wait_ge(gl_ready, 4 * (G_GEN["in4"] + 1))
            act.dma_start(posi[:, :], pos).then_inc(M("pos_in"), 16)
            act.dma_start(rt_d[:, :, :], decay).then_inc(M("decay_in"), 16)

            def ret_gate(j):
                u = PLAN.at["gret"][1] + j
                done(u)
                for t in range(2):
                    k = 2 * j + t
                    A(sgt[:, k, :], banks(u)[:, t, :], ACT.Sigmoid, bias=col("mgb", k)).then_inc(*own.sig(rel["act"] if t else None))

            for g in range(2):
                for j in range(4):
                    u = u0 + 6 * g + j
                    done(u)
                    if j < 2:
                        n = 2 * g + j
                        if n:
                            act.wait_ge(M("rot_done"), 2 * n)
                        ins = A(rt_f[:, :, :], banks(u), ACT.Copy, scale=1.0 if j == 0 else P ** -0.5)
                    else:
                        ins = A(rt_v[:, j - 2].rearrange("p (b s) n -> p b (s n)", b=2), banks(u), ACT.Copy)
                    ins.then_inc(*own.sig(rel["act"]))
                    if j == 0 and g == 0:
                        act.wait_ge(M("rot_in"), 1)
                        A(sinf[:, :], sinf[:, :], ACT.Sin).then_inc(*own.sig(M("trig")))
                        A(cosf[:, :], cosf[:, :], ACT.Sin).then_inc(*own.sig(M("trig")))
                for hh in range(2):
                    hd = 2 * g + hh
                    act.wait_ge(M("rav"), 4 * (hd + 1))
                    if hd:
                        act.wait_ge(xl_ready, 4 * X_GEN["ret"] + hd)
                    A(rt_o[:, :, :], mix[:, 2:4, :], ACT.Copy).then_inc(*own.sig(M("ro_copied")))
                    A(rt_o2[:, :, :], mix[:, 2:4, :], ACT.Square).then_inc(*own.sig(M("ro_copied")))
                    for j in ((hh,) if g == 0 else (0, 1) if hh == 0 else ()):
                        done(u0 + 6 * g + 4 + j)
                        if g and j == 0:
                            act.wait_ge(M("z_ret"), 2)
                        A(rt_g[:, j], banks(u0 + 6 * g + 4 + j), ACT.Silu).then_inc(*own.sig(rel["act"]))
                    if hd == 3:
                        ret_gate(0)
                        ret_gate(1)
                    act.wait_ge(M("rst"), hd + 1)
                    A(rt_m[:, :], mix[:, 0, :], ACT.Copy, scale=1.0 / 256).then_inc(*own.sig(M("r_mean")))
                    A(rt_rs[:, :], mix[:, 0, :], ACT.Square, scale=1.0 / 256).then_inc(*own.sig(M("r_mean")))
                    act.wait_ge(M("rvar"), hd + 1)
                    A(rt_rs[:, :], rt_rs[:, :], ACT.Sqrt).then_inc(*own.sig(M("rstdd")))
                    act.wait_ge(M("z_ret"), hd + 1)
                    A(xh[:, 2 * hd:2 * hd + 2, :], rt_o[:, :, :], ACT.Copy).then_inc(*own.sig(xh_ready))
            act.wait_ge(xl_ready, 4 * (X_GEN["ret"] + 1))
            ret_gate(2)
            ret_gate(3)
            s0, u0 = PLAN.at["xlru"]
            for j in range(4):
                done(u0 + j)
                for t in range(2):
                    k = 2 * j + t
                    A(xc[:, k, :], banks(u0 + j)[:, t, :], ACT.Identity, scale=col("lconvw", 24 + k), bias=col("lconvb", k))\
                        .then_inc(*own.sig(M("tap")))
                act.wait_ge(rel["dve"], PLAN.released(u0 + j)[1])
                A(xh[:, 2 * j:2 * j + 2, :], xc[:, 2 * j:2 * j + 2, :], ACT.Copy).then_inc(*own.sig(xh_ready))
            s0, u0 = PLAN.at["lru"]
            act.wait_ge(rel["dve"], PLAN.released(PLAN.at["reto"][1] + 3)[1])
            for n in range(4):
                done(u0 + 3 * n)
                for t in range(2):
                    k = 2 * n + t
                    A(sgt[:, k, :], banks(u0 + 3 * n)[:, t, :], ACT.Sigmoid, bias=col("mgb", 8 + k))\
                        .then_inc(*own.sig(rel["act"] if t else None))
                for s, (buf, b) in enumerate(((lr, "br"), (li, "bi"))):
                    done(u0 + 3 * n + 1 + s)
                    if n:
                        act.wait_ge(M("hl_done"), 2 * n)
                    for t in range(2):
                        A(buf[:, t, :], banks(u0 + 3 * n + 1 + s)[:, t, :], ACT.Sigmoid, bias=col(b, 2 * n + t))\
                            .then_inc(*own.sig(rel["act"] if t else None))
                mine()
                for t in range(2):
                    k = 2 * n + t
                    A(la[:, t, :], lr[:, t, :], ACT.Exp, scale=small[:, 36 + k:37 + k]).then_inc(*own.sig())
                    A(lu[:, t, :], lr[:, t, :], ACT.Tanh, scale=small[:, 28 + k:29 + k]).then_inc(*own.sig(M("u_act")))
                act.wait_ge(M("b_done"), 3 * n + 2)
                A(lu[:, :, :], lu[:, :, :], ACT.Sqrt).then_inc(*own.sig(M("r_act")))
            s0, u0 = PLAN.at["ylru"]
            for j in range(4):
                done(u0 + j)
                if j:
                    act.wait_ge(xl_ready, 4 * X_GEN["lru"] + j)
                else:
                    act.wait_ge(M("hl_done"), 8)
                A(lr[:, :, :], banks(u0 + j), ACT.Gelu_apprx_tanh).then_inc(*own.sig(rel["act"]))
                act.wait_ge(M("z_lru"), j + 1)
                A(xh[:, 2 * j:2 * j + 2, :], lr[:, :, :], ACT.Copy).then_inc(*own.sig(xh_ready))
            for j in range(4):
                act.wait_ge(M("mixed"), j + 1)
                A(gh[:, 2 * j:2 * j + 2, :], mixt[:, 2 * j:2 * j + 2, :], ACT.Copy).then_inc(*own.sig(gh_ready))
            s0, u0 = PLAN.at["wout"]
            for j in range(4):
                ln_squares(u0 + j, j, 9)
            rms_apply(9, "norm2", xh, xh_ready)
            s0, u0 = PLAN.at["ffnb"]
            base = PLAN.released(u0)[1] - 1

            def third(q):
                for j in range(4):
                    act.wait_ge(unit_done, q * 12 + (u0 + 2 * j + 1) if q is not None else u0 + 2 * j + 25)
                    act.wait_ge(gl_ready, q * 4 + (G_GEN["ffnb"] * 4 + j) if q is not None else G_GEN["ffnb"] * 4 + 8 + j)
                    for t in range(2):
                        k = 2 * j + t
                        w = vec[:, bass.ds(q * 8 + (VEC["fconvw"] + 48 + k), 1)] if q is not None else col("fconvw", 64 + k)
                        b = vec[:, bass.ds(q * 8 + (VEC["fconvb"] + k), 1)] if q is not None else col("fconvb", 16 + k)
                        A(cv[:, t, :], banks(u0 + 2 * j)[:, t, :], ACT.Identity, scale=w, bias=b).then_inc(*own.sig(M("tap2")))
                    act.wait_ge(rel["dve"], q * 12 + (base + 2 * j + 1) if q is not None else base + 2 * j + 25)
                    A(cv[:, :, :], cv[:, :, :], ACT.Gelu_apprx_tanh).then_inc(*own.sig(M("gelu2")))
                    act.wait_ge(rel["dve"], q * 12 + (base + 2 * j + 2) if q is not None else base + 2 * j + 26)
                    A(gh[:, 2 * j:2 * j + 2, :], hid2[:, :, :], ACT.Copy).then_inc(*own.sig(gh_ready))

            with act.Fori(0, 2) as q:
                own.enter(q, {M("tap2"): 8, M("gelu2"): 4, gh_ready: 4})
                third(q)
                own.leave(2)
            third(None)
            for j in range(4):
                ln_squares(u0 + 32 + j, j, 10)
            rms_apply(10, "normf", None, None)

        @block.vector
        def _(dve):
            own = Own(dve_own)
            V = nc.vector

            def mine():
                dve.wait_ge(*own.last())

            def banks(u):
                return proj[:, 2 * (u % 2):2 * (u % 2) + 2, :]

            def done(u):
                dve.wait_ge(unit_done, u + 1)

            def low_part(lo, full, hi, sem, hi_sem, hi_value):
                dve.wait_ge(hi_sem, hi_value)
                V.tensor_tensor(lo, full, hi.bitcast(F32), ALU.subtract).then_inc(*own.sig(sem))

            V.memset(ones[:, :], 1.0).then_inc(*own.sig())
            V.memset(small[:, :], 0.0).then_inc(*own.sig())
            mine()
            V.memset(small[:, 252:253], RMS_EPS).then_inc(*own.sig())
            V.memset(rb[32:33, :], 1.0).then_inc(*own.sig(M("start_dve")))
            for t in range(4):
                p2 = slice(2 * t, 2 * t + 2)
                low_part(gl[:, p2, :], h[:, p2, :], gh[:, p2, :], gl_ready, gh_ready, t + 1)
            dve.wait_ge(loaded, 16 * LOADS)
            mine()
            lam = col("lam", 0, 8)[0:64, :].rearrange("p (a b) -> p a b", b=2)
            V.tensor_tensor(small[0:64, 0:4], lam[:, :, 0], lam[:, :, 1], ALU.mult).then_inc(*own.sig(M("lamprod")))
            lb = lambda j: col("lb", 8 * j, 8)
            mxl = small[:, 52:60]
            V.tensor_tensor(mxl, lb(0), lb(1), ALU.max).then_inc(*own.sig())
            for j in (2, 3):
                mine()
                V.tensor_tensor(mxl, mxl, lb(j), ALU.max).then_inc(*own.sig())
            mine()
            for j in range(4):
                V.tensor_tensor(small[:, 64 + 8 * j:72 + 8 * j], lb(j), mxl, ALU.subtract).then_inc(*own.sig(M("start_dve") if j == 3 else None))
            mine()
            V.tensor_scalar(h[:, :, :], h[:, :, :], ALPHA, None, ALU.mult).then_inc(*own.sig())
            dve.wait_ge(M("lamexp"), 1)
            lx = small[:, 4:8].rearrange("p (a b) -> p a b", b=2)
            V.tensor_tensor(small[:, 8:10], lx[:, :, 1], lx[:, :, 0], ALU.subtract).then_inc(*own.sig())
            mine()
            for d in range(2):
                V.tensor_scalar(small[:, 8 + d:9 + d], small[:, 8 + d:9 + d], LAM_INIT[d], None, ALU.subtract).then_inc(*own.sig())
                V.tensor_scalar(small[:, 10 + d:11 + d], col("subln", d), 1.0 - LAM_INIT[d], None, ALU.mult).then_inc(*own.sig())
            dve.wait_ge(M("lamexp"), 2)
            ex = lambda j: small[:, 64 + 8 * j:72 + 8 * j]
            V.tensor_tensor(mxl, ex(0), ex(1), ALU.add).then_inc(*own.sig())
            for j in (2, 3):
                mine()
                V.tensor_tensor(mxl, mxl, ex(j), ALU.add).then_inc(*own.sig())
            mine()
            V.reciprocal(mxl, mxl).then_inc(*own.sig())
            mine()
            V.tensor_tensor(small[:, 12:20], ex(1), mxl, ALU.mult).then_inc(*own.sig())
            mine()
            V.tensor_scalar(small[:, 20:28], small[:, 12:20], -1.0, 1.0, ALU.mult, ALU.add).then_inc(*own.sig())
            dve.wait_ge(M("lamexp"), 3)
            e_, s_, s2_, p_ = small[:, 44:52], small[:, 52:60], small[:, 160:168], small[:, 168:176]
            V.tensor_scalar(s_, e_, 2.0, None, ALU.add).then_inc(*own.sig())
            mine()
            V.reciprocal(s_, s_).then_inc(*own.sig())
            mine()
            V.tensor_tensor(s_, s_, e_, ALU.mult).then_inc(*own.sig())
            mine()
            V.tensor_tensor(s2_, s_, s_, ALU.mult).then_inc(*own.sig())
            mine()
            V.tensor_scalar(p_, s2_, 1.0 / 15, None, ALU.mult).then_inc(*own.sig())
            for c in (13, 11, 9, 7, 5, 3):
                mine()
                V.scalar_tensor_tensor(p_, p_, 1.0 / c, s2_, ALU.add, ALU.mult).then_inc(*own.sig())
            mine()
            V.scalar_tensor_tensor(p_, p_, 1.0, s_, ALU.add, ALU.mult).then_inc(*own.sig())
            mine()
            V.tensor_scalar(e_, col("lamb", 0, 8), -8.0, 0.0, ALU.mult, ALU.max).then_inc(*own.sig())
            mine()
            V.scalar_tensor_tensor(small[:, 28:36], p_, 16.0, e_, ALU.mult, ALU.add).then_inc(*own.sig())
            mine()
            V.tensor_scalar(small[:, 36:44], small[:, 28:36], -1.0, None, ALU.mult).then_inc(*own.sig())

            def add_unit(u, j):
                done(u)
                mine()
                p2 = slice(2 * j, 2 * j + 2)
                V.tensor_tensor(h[:, p2, :], h[:, p2, :], banks(u), ALU.add).then_inc(*own.sig(rel["dve"]))

            def sums(j, l, with_mean=True):
                def add(total, pair, sem=None):
                    if j < 3:
                        mine()
                        V.tensor_tensor(total[:, :, :], pair[0], pair[1], ALU.add).then_inc(*own.sig(None if j < 3 and sem is M("s1_done") else sem))
                        if j == 2:
                            mine()
                            V.tensor_tensor(total[:, 0, :], total[:, 0, :], total[:, 1, :], ALU.add).then_inc(*own.sig())
                    else:
                        for t in range(2):
                            mine()
                            V.tensor_tensor(total[:, 0, :], total[:, 0, :], pair[1][:, t, :], ALU.add).then_inc(*own.sig(sem if t else None))

                if with_mean and j:
                    add(s1, (h[:, 0:2, :] if j == 1 else s1[:, :, :], h[:, 2 * j:2 * j + 2, :]), M("s1_done"))
                if j:
                    dve.wait_ge(M("sq_done"), 4 * l + j + 1)
                    add(s2, (sq[:, 0] if j == 1 else s2[:, :, :], sq[:, j % 2]), M("s2_done"))

            def rstd_from(l, eps):
                mine()
                V.tensor_scalar(rstd[:, :], rstd[:, :], 0.0, eps, ALU.max, ALU.add).then_inc(*own.sig(M("msq_read")))
                dve.wait_ge(M("rstd_done"), l + 1)
                V.reciprocal(rstd[:, :], rstd[:, :]).then_inc(*own.sig())

            def ln_apply(l, gen):
                def centre(j):
                    p2 = slice(2 * j, 2 * j + 2)
                    mine()
                    V.tensor_tensor(h[:, p2, :], h[:, p2, :], mean[:, :].rearrange("p (a s) -> p a s", a=1).broadcast_to([P, 2, S]),
                                    ALU.subtract).then_inc(*own.sig())

                dve.wait_ge(M("mean_read"), 2 * l + 1)
                centre(0)
                dve.wait_ge(M("stats"), 2 * (l + 1))
                dve.wait_ge(M("mean_read"), 2 * l + 2)
                V.scalar_tensor_tensor(rstd[:, :], mix[:, 1, :], 1.0 / D, msq[:, :], ALU.mult, ALU.subtract).then_inc(*own.sig(M("msq_read")))
                mine()
                V.tensor_scalar(rstd[:, :], rstd[:, :], 0.0, LN_EPS, ALU.max, ALU.add).then_inc(*own.sig(M("msq_read")))
                centre(1)
                dve.wait_ge(M("rstd_done"), l + 1)
                V.reciprocal(rstd[:, :], rstd[:, :]).then_inc(*own.sig())
                c = 8 * l
                for k in range(8):
                    if k >= 2:
                        dve.wait_ge(*((xh_ready, 4 * gen + (k - 2) // 2 + 1) if k % 2 else (M("ln_h"), 4 * l + (k - 2) // 2 + 1)))
                    mine()
                    V.tensor_tensor(tln[:, k % 2, :], h[:, k, :], rstd[:, :], ALU.mult).then_inc(*own.sig(M("ln_u")))
                    mine()
                    V.tensor_scalar(h[:, k, :], tln[:, k % 2, :], col("ln_g", c + k), col("ln_b", c + k), ALU.mult, ALU.add)\
                        .then_inc(*own.sig(M("ln_full")))
                    if k in (1, 3):
                        centre(k // 2 + 2)
                dve.wait_ge(xl_ready, 4 * (gen + 1))
                own.others(xl_ready, 4)

            def scale_h(c=slice(0, KT)):
                mine()
                V.tensor_scalar(h[:, c, :], h[:, c, :], ALPHA, None, ALU.mult).then_inc(*own.sig())

            def rms_apply(l, name, out_hi, out_lo, lo_sem):
                dve.wait_ge(M("stats"), 16 + l - 8 + 1)
                V.tensor_scalar(rstd[:, :], mix[:, 1, :], 1.0 / D, None, ALU.mult).then_inc(*own.sig(M("msq_read")))
                rstd_from(l, RMS_EPS)
                gen = 4 * (G_GEN["in4"] if l == 8 else X_GEN["rms2"])

                def high(k):
                    if out_hi is None:
                        return M("final_out"), k + 1
                    return ((gh_ready if l == 8 else xh_ready), gen + k // 2 + 1) if k % 2 else (M("ln_h"), 32 + 4 * (l - 8) + k // 2 + 1)

                def low(k):
                    dve.wait_ge(*high(k))
                    V.scalar_tensor_tensor(out_lo[:, k, :], tln[:, k % 2, :], col(name, k), out_hi[:, k, :].bitcast(F32), ALU.mult, ALU.subtract)\
                        .then_inc(*own.sig(lo_sem if k % 2 else None))

                for k in range(8):
                    if k >= 2:
                        dve.wait_ge(*high(k - 2))
                    mine()
                    V.tensor_tensor(tln[:, k % 2, :], h[:, k, :], rstd[:, :], ALU.mult).then_inc(*own.sig(M("ln_u")))
                    if k and out_hi is not None:
                        low(k - 1)
                if out_hi is not None:
                    low(7)

            def head_norm(n, buf, on):
                dve.wait_ge(M("o_rstd"), n + 1)
                mine()
                V.tensor_tensor(on[:, :], mix[:, 3, :], buf[:, :], ALU.mult).then_inc(*own.sig(M("o_norm")))

            def da_mixer(d, layer):
                s0, u0 = PLAN.at[f"mix{layer}"]

                def mask(k):
                    it, hd, qb = 32 * d + k, k // 4, k % 4
                    w = (qb + 1) * P
                    dve.wait_ge(M("scores"), it + 1)
                    if qb == 0:
                        dve.wait_ge(M(f"bias_in{hd % 2}"), 16 * (4 * d + hd // 2 + 1))
                    mine()
                    for mp in range(2):
                        c = 100 + 2 * (k % 2) + mp
                        V.tensor_tensor_reduce(out=da_s[:, k % 2, mp, 0:w], in0=mix[:, mp, 0:w], in1=da_b[:, hd % 2, mp, S - w:S],
                                               scale=1.0, scalar=-3.0e38, op0=ALU.add, op1=ALU.max, accum_out=small[:, c:c + 1])\
                            .then_inc(*own.sig(M("masked")))
                    mine()
                    c = 2 * (k % 2)
                    V.tensor_scalar(small[:, 104 + c:106 + c], small[:, 100 + c:102 + c], -1.0, None, ALU.mult).then_inc(*own.sig(M("negmax")))

                def coef(k):
                    it = 32 * d + k
                    c = 2 * (k % 2)
                    dve.wait_ge(M("expd"), 2 * (it + 1))
                    mine()
                    V.reciprocal(small[:, 176 + c:178 + c], small[:, 108 + c:110 + c]).then_inc(*own.sig())
                    mine()
                    V.tensor_scalar(small[:, 114 + c:115 + c], small[:, 177 + c:178 + c], small[:, 8 + d:9 + d], None, ALU.mult).then_inc(*own.sig(M("coef")))

                def combine(k):
                    it, qb = 32 * d + k, k % 4
                    w = (qb + 1) * P
                    c = 2 * (k % 2)
                    dve.wait_ge(M("second"), it + 1)
                    if it >= 2:
                        dve.wait_ge(M("transposed"), it - 1)
                    V.scalar_tensor_tensor(da_a[:, k % 2, 0:w], da_s[:, k % 2, 0, 0:w], small[:, 176 + c:177 + c], da_t[:, k % 2, 0:w],
                                           ALU.mult, ALU.add).then_inc(*own.sig(M("attn")))

                def head_lo(hd):
                    dve.wait_ge(xh_ready if hd % 2 else M("hi_even"),
                                4 * X_GEN[f"mix{layer}"] + hd // 2 + 1 if hd % 2 else {0: 0, 3: 8}[layer] + hd // 2 + 1)
                    V.scalar_tensor_tensor(xl[:, hd, :], post_on[:, :], small[:, 10 + d:11 + d], xh[:, hd, :].bitcast(F32), ALU.mult, ALU.subtract)\
                        .then_inc(*own.sig(xl_ready if hd % 2 else None))

                for k in range(32 + 4):
                    if k < 32:
                        mask(k)
                    if 1 <= k < 33:
                        coef(k - 1)
                    if k >= 7 and k % 4 == 3:
                        head_norm(post_base(layer) + (k - 7) // 4, post_rs, post_on)
                    if 1 <= k < 33:
                        combine(k - 1)
                    if k >= 8 and k % 4 == 0:
                        head_lo((k - 8) // 4)
                head_lo(7)

            def hg_mixer(layer):
                s0, u0 = PLAN.at[f"mix{layer}"]

                def forget(g):
                    dve.wait_ge(rel["act"], PLAN.released(u0 + 4 * g)[1])
                    mine()
                    for t in range(2):
                        c = 2 * g + t
                        V.tensor_scalar(hg_f[:, g % 2, t, :], hg_f[:, g % 2, t, :], small[:, 20 + c:21 + c], small[:, 12 + c:13 + c], ALU.mult, ALU.add).then_inc(*own.sig(M("hg_f")))
                    mine()
                    for t in range(2):
                        V.tensor_scalar(hg_k[:, g % 2, t, :], hg_f[:, g % 2, t, :], -1.0, 1.0, ALU.mult, ALU.add).then_inc(*own.sig(M("hg_lf")))

                def scan(g):
                    dve.wait_ge(M("hg_ln"), g + 1)
                    mine()
                    for t in range(2):
                        V.tensor_tensor_scan(hg_f[:, g % 2, t, :], reset[:, :], hg_f[:, g % 2, t, :], 0.0, ALU.mult, ALU.add).then_inc(*own.sig(M("hg_ready")))

                def halves(ap, b):
                    v = ap.rearrange("p (n c) -> p n c", c=2 * b)
                    return v[:, :, 0:b], v[:, :, b:2 * b], v[:, :, b - 1:b].broadcast_to([P, S // (2 * b), b])

                def diff(hd, j):
                    n, b = 7 * hd + j - 1, HG_LEVELS[j - 1]
                    lo, up, at = halves(hg_f[:, hd // 2 % 2, hd % 2, :], b)
                    elo, eup, _ = halves(hg_e[:, n % 2, :], b)
                    mine()
                    V.tensor_tensor(elo, at, lo, ALU.subtract).then_inc(*own.sig())
                    V.tensor_tensor(eup, up, at, ALU.subtract).then_inc(*own.sig(M("hg_diff")))

                def product(hd, j):
                    n, b = 7 * hd + j - 1, HG_LEVELS[j - 1]
                    g, t = hd // 2 % 2, hd % 2
                    dve.wait_ge(M("hg_exp"), n + 1)
                    if j == 1:
                        dve.wait_ge(rel["act"], PLAN.released(u0 + 4 * (hd // 2) + 1)[1])
                    if n >= 2:
                        n2 = n - 2
                        dve.wait_ge(M("hg_sc"), 9 * (n2 // 7) + n2 % 7 + 2)
                    mine()
                    elo, eup, _ = halves(hg_e[:, n % 2, :], b)
                    plo_, pup, _ = halves(hg_p[:, n % 2, :], b)
                    klo, _, _ = halves(hg_k[:, g, t, :], b)
                    _, qup, _ = halves(hg_q[:, g, t, :], b)
                    V.tensor_tensor(plo_, elo, klo, ALU.mult).then_inc(*own.sig())
                    V.tensor_tensor(pup, eup, qup, ALU.mult).then_inc(*own.sig(M("hg_prod")))

                def take(hd, j):
                    it = 8 * hd + j
                    dve.wait_ge(M("hg_sc"), 9 * hd + j + 1)
                    bank = mix[:, it % 2, :].rearrange("p (a b) -> p a b", a=4)
                    if j == 0:
                        if hd:
                            dve.wait_ge(M("hg_av"), hd)
                        V.tensor_tensor(hg_a[:, :, :], bank, ident[:, :].rearrange("p (a b) -> p a b", a=1).broadcast_to([P, 4, P]), ALU.mult)\
                            .then_inc(*own.sig(M("hg_pick")))
                    else:
                        mine()
                        V.copy_predicated(hg_a[:, :, :], pick[:, j - 1:j, :].broadcast_to([P, 4, P]), bank).then_inc(*own.sig(M("hg_pick")))

                def far_diff(hd):
                    G_ = hg_f[:, hd // 2 % 2, hd % 2, :].rearrange("p (t c) -> p t c", t=4)
                    if hd:
                        dve.wait_ge(M("hg_sc"), 9 * hd)
                    mine()
                    V.tensor_tensor(hg_kd[:, 0:4, :], G_[:, :, P - 1:P].broadcast_to([P, 4, P]), G_, ALU.subtract).then_inc(*own.sig(M("hg_fardiff")))

                def far_products(hd):
                    g, t = hd // 2 % 2, hd % 2
                    q_ = hg_q[:, g, t, :].rearrange("p (t c) -> p t c", t=4)
                    k_ = hg_k[:, g, t, :].rearrange("p (t c) -> p t c", t=4)
                    dve.wait_ge(M("hg_farexp"), hd + 1)
                    mine()
                    V.tensor_tensor(hg_kd[:, 0:3, :], hg_kd[:, 0:3, :], k_[:, 0:3, :], ALU.mult).then_inc(*own.sig())
                    V.tensor_tensor(hg_qd[:, 0:2, :], hg_x[:, 1:3, :], q_[:, 1:3, :], ALU.mult).then_inc(*own.sig())
                    V.tensor_tensor(hg_qd[:, 3, :], hg_x[:, 3, :], q_[:, 3, :], ALU.mult).then_inc(*own.sig())
                    mine()
                    V.tensor_scalar(hg_kd[:, 3, :], hg_kd[:, 0, :], hg_x[:, 1, P - 1:P], None, ALU.mult).then_inc(*own.sig())
                    V.tensor_scalar(hg_qd[:, 2, :], hg_qd[:, 3, :], hg_x[:, 2, P - 1:P], None, ALU.mult).then_inc(*own.sig(M("hg_fark")))

                def post(hd):
                    n = post_base(layer) + hd
                    head_norm(n, hrs, hon)
                    mine()
                    V.scalar_tensor_tensor(hon[:, :], hon[:, :], col("gnorm"), hg_g[:, hd // 2 % 2, hd % 2, :], ALU.mult, ALU.mult)\
                        .then_inc(*own.sig(M("z_done")))

                def head_lo(hd):
                    dve.wait_ge(xh_ready if hd % 2 else M("hi_even"),
                                4 * X_GEN[f"mix{layer}"] + hd // 2 + 1 if hd % 2 else 4 + hd // 2 + 1)
                    V.tensor_tensor(xl[:, hd, :], hon[:, :], xh[:, hd, :].bitcast(F32), ALU.subtract)\
                        .then_inc(*own.sig(xl_ready if hd % 2 else None))

                forget(0)
                scan(0)
                for k in range(81):
                    hd, j = k // 10, k % 10
                    g, kk = k // 20, k % 20
                    if k < 80 and j < 7:
                        diff(hd, j + 1)
                    if 1 <= j <= 7:
                        product(hd, j)
                    if j == 0 and hd:
                        dve.wait_ge(rel["act"], PLAN.released(u0 + 4 * ((hd - 1) // 2) + 3)[1])
                        post(hd - 1)
                    if 1 <= j <= 8:
                        take(hd, j - 1)
                    if j == 5:
                        far_diff(hd)
                    if j == 7:
                        far_products(hd)
                    if j == 3 and hd:
                        head_lo(hd - 1)
                    if k < 60 and kk == 6:
                        forget(g + 1)
                    if k < 60 and kk == 8:
                        scan(g + 1)
                head_lo(7)

            def sw_mixer(layer):
                xg = X_GEN[f"mix{layer}"]

                def mask(k):
                    g, b = k // 4, k % 2
                    kn = sw_blocks(k % 4) * P
                    dve.wait_ge(M("sw_scores"), k + 1)
                    if k % 4 == 0:
                        dve.wait_ge(M(f"sw_bias{g % 2}"), 16 * (g // 2 + 1))
                    if k >= 2:
                        dve.wait_ge(M("sw_transposed"), sw_q_index(k - 2, sw_blocks((k - 2) % 4) - 1) + 1)
                    mine()
                    for hd in range(4):
                        V.tensor_tensor_reduce(out=sw_s[:, b, hd, 0:kn], in0=mix[:, hd % 2, (hd // 2) * 256:(hd // 2) * 256 + kn],
                                               in1=sw_b[:, g % 2, hd, 256 - kn:256], scale=1.0, scalar=-3.0e38, op0=ALU.add, op1=ALU.max,
                                               accum_out=small[:, 116 + 4 * b + hd:117 + 4 * b + hd]).then_inc(*own.sig(M("sw_masked")))
                    mx, nm, es = (small[:, c + 4 * b:c + 4 * b + 4] for c in (116, 124, 140))
                    sink = col("sinks", 4 * g, 4)
                    mine()
                    V.tensor_tensor(mx, mx, sink, ALU.max).then_inc(*own.sig())
                    mine()
                    V.tensor_tensor(es, sink, mx, ALU.subtract).then_inc(*own.sig())
                    V.tensor_scalar(nm, mx, -1.0, None, ALU.mult).then_inc(*own.sig(M("sw_negmax")))

                def normal(k):
                    b = k % 2
                    kn = sw_blocks(k % 4) * P
                    dve.wait_ge(M("sw_expd"), k + 1)
                    ss, es = (small[:, c + 4 * b:c + 4 * b + 4] for c in (132, 140))
                    r = small[:, 148 + 4 * b:152 + 4 * b]
                    mine()
                    V.tensor_tensor(r, ss, es, ALU.add).then_inc(*own.sig())
                    mine()
                    V.reciprocal(r, r).then_inc(*own.sig())
                    mine()
                    s_ = sw_s[:, b, :, 0:kn]
                    V.tensor_tensor(s_, s_, r.rearrange("p (a b) -> p a b", b=1).broadcast_to([P, 4, kn]), ALU.mult).then_inc(*own.sig(M("sw_attn")))

                def lo(k):
                    g, n = k // 4, k % 4
                    dve.wait_ge(*((xh_ready, 4 * xg + g + 1) if n == 3 else (M("sw_hi"), 3 * g + n + 1)))
                    c = slice(n * P, (n + 1) * P)
                    V.tensor_tensor(xl[:, 2 * g:2 * g + 2, c], sw_o[:, k % 2],
                                    xh[:, 2 * g:2 * g + 2, c].bitcast(F32), ALU.subtract)\
                        .then_inc(*own.sig(xl_ready if n == 3 else M("sw_lo")))

                for k in range(16 + 4):
                    if k < 16:
                        mask(k)
                    if 1 <= k < 17:
                        normal(k - 1)
                    if 3 <= k < 19:
                        lo(k - 3)

            def ffn(layer):
                s0, u0 = PLAN.at[f"ffn{layer}"]
                r0, g0 = 16 * layer, 4 * G_GEN[f"ffn{layer}"]

                def quarter(q, downs=True):
                    for j in range(4):
                        dve.wait_ge(M("relu_done"), q * 4 + (r0 + j + 1) if q is not None else r0 + 13 + j)
                        if own.at is not None:
                            mine()
                        V.scalar_tensor_tensor(hid[:, :, :], banks(u0 + j), 0.0, rl[:, :, :], ALU.max, ALU.mult).then_inc(*own.sig(rel["dve"]))
                        dve.wait_ge(gh_ready, q * 4 + (g0 + j + 1) if q is not None else g0 + 13 + j)
                        V.tensor_tensor(gl[:, 2 * j:2 * j + 2, :], hid[:, :, :], gh[:, 2 * j:2 * j + 2, :].bitcast(F32), ALU.subtract)\
                            .then_inc(*own.sig(gl_ready))
                    for j in range(4):
                        p2 = slice(2 * j, 2 * j + 2)
                        dve.wait_ge(unit_done, q * 8 + (u0 + 4 + j + 1) if q is not None else u0 + 29 + j)
                        mine()
                        V.tensor_tensor(h[:, p2, :], h[:, p2, :], banks(u0 + 4 + j), ALU.add).then_inc(*own.sig(rel["dve"]))
                        if q is None:
                            sums(j, 2 * layer + 1)

                mine()
                with dve.Fori(0, 3) as q:
                    own.enter(q, {rel["dve"]: 8, gl_ready: 4})
                    quarter(q)
                    mine()
                    own.leave(3)
                quarter(None)

            for layer in range(NL):
                if layer % 3 == 0:
                    da_mixer(layer // 3, layer)
                elif layer == 1:
                    hg_mixer(layer)
                else:
                    sw_mixer(layer)
                s0, u0 = PLAN.at[f"out{layer}"]
                for j in range(4):
                    add_unit(u0 + j, j)
                    sums(j, 2 * layer)
                ln_apply(2 * layer, X_GEN[f"ln1{layer}"])
                scale_h()
                dve.wait_ge(M("p_hi"), layer + 1)
                V.tensor_tensor(plo[:, :, :], pf[:, :, :], ph[:, :, :].bitcast(F32), ALU.subtract).then_inc(*own.sig(M("p_lo")))
                ffn(layer)
                ln_apply(2 * layer + 1, X_GEN[f"ln2{layer}"])
                s0, u0 = PLAN.at[f"gate{layer}"]
                for j in range(4):
                    p2 = slice(2 * j, 2 * j + 2)
                    dve.wait_ge(rel["act"], PLAN.released(u0 + j)[1])
                    mine()
                    V.tensor_tensor(sg[:, j % 2], sg[:, j % 2], po[:, p2, :], ALU.mult).then_inc(*own.sig())
                    mine()
                    V.tensor_tensor(h[:, p2, :], h[:, p2, :], sg[:, j % 2], ALU.add).then_inc(*own.sig(M("h_new")))
                    if layer < NL - 1:
                        low_part(gl[:, p2, :], h[:, p2, :], gh[:, p2, :], gl_ready, gh_ready, 4 * G_GEN[f"in{layer + 1}"] + j + 1)
                        scale_h(p2)
                    else:
                        sums(j, 8, with_mean=False)

            rms_apply(8, "norm1", gh, gl, gl_ready)
            dve.wait_ge(M("pos_in"), 16)
            V.tensor_copy(ang[:, :], posi[:, :]).then_inc(*own.sig())
            mine()
            V.tensor_scalar(ang[:, :], ang[:, :], col("invf"), None, ALU.mult).then_inc(*own.sig())
            C1 = 6.28125
            C2 = float(np.float32(math.floor((2 * math.pi - C1) * 2 ** 21) / 2 ** 21))
            C3 = 2 * math.pi - C1 - C2
            MAGIC = 1.5 * 2.0 ** 23
            for dst, quarter_turn in ((sinf, 0.0), (cosf, 0.25)):
                mine()
                V.tensor_scalar(turn[:, :], ang[:, :], 1.0 / (2 * math.pi), quarter_turn, ALU.mult, ALU.add).then_inc(*own.sig())
                mine()
                V.tensor_scalar(turn[:, :], turn[:, :], MAGIC, None, ALU.add).then_inc(*own.sig())
                mine()
                V.tensor_scalar(turn[:, :], turn[:, :], MAGIC, None, ALU.subtract).then_inc(*own.sig())
                src = ang
                for c in (C1, C2, C3):
                    mine()
                    V.scalar_tensor_tensor(dst[:, :], turn[:, :], -c, src[:, :], ALU.mult, ALU.add).then_inc(*own.sig())
                    src = dst
                mine()
                V.tensor_scalar(dst[:, :], dst[:, :], quarter_turn * 2 * math.pi, 3.1415925, ALU.add, ALU.min).then_inc(*own.sig())
                mine()
                V.tensor_scalar(dst[:, :], dst[:, :], -3.1415925, None, ALU.max).then_inc(*own.sig(M("rot_in") if quarter_turn else None))

            s0, u0 = PLAN.at["ret"]
            for g in range(2):
                for j in range(2):
                    n = 2 * g + j
                    if n == 0:
                        dve.wait_ge(M("trig"), 2)
                    dve.wait_ge(rel["act"], PLAN.released(u0 + 6 * g + j)[1])
                    dst = rt_q if j == 0 else rt_k
                    for hh in range(2):
                        mine()
                        V.tensor_tensor(rt_t[:, 0, :], rt_f[:, hh, :], cosf[:, :], ALU.mult).then_inc(*own.sig())
                        dve.wait_ge(M("rot_mm"), n + 1)
                        V.tensor_tensor(rt_t[:, 1, :], mix[:, hh, :], sinf[:, :], ALU.mult).then_inc(*own.sig())
                        mine()
                        V.tensor_tensor(dst[:, hh, :], rt_t[:, 0, :], rt_t[:, 1, :], ALU.add).then_inc(*own.sig(M("rot_done")))
                for hh in range(2):
                    hd = 2 * g + hh
                    for kb in range(4):
                        n = 4 * hd + kb
                        w = S - kb * P
                        dve.wait_ge(M("rsc"), n + 1)
                        if n == 0:
                            dve.wait_ge(M("decay_in"), 16)
                        if n >= 2:
                            dve.wait_ge(M("rav"), n - 1)
                        V.tensor_tensor(rt_s[:, n % 2, 0:w], mix[:, n % 2, 0:w], rt_d[:, hd, 0:w], ALU.mult).then_inc(*own.sig(M("rmul")))
                    dve.wait_ge(M("rst"), hd + 1)
                    dve.wait_ge(M("r_mean"), 2 * (hd + 1))
                    V.scalar_tensor_tensor(rt_rs[:, :], mix[:, 1, :], 1.0 / 256, rt_rs[:, :], ALU.mult, ALU.subtract).then_inc(*own.sig(M("rn_done")))
                    mine()
                    V.tensor_scalar(rt_rs[:, :], rt_rs[:, :], 0.0, RMS_EPS, ALU.max, ALU.add).then_inc(*own.sig(M("rvar")))
                    dve.wait_ge(M("rstdd"), hd + 1)
                    V.reciprocal(rt_rs[:, :], rt_rs[:, :]).then_inc(*own.sig())
                    for t in range(2):
                        V.tensor_tensor(rt_o[:, t, :], rt_o[:, t, :], rt_m[:, :], ALU.subtract).then_inc(*own.sig())
                    mine()
                    for t in range(2):
                        V.tensor_tensor(rt_o[:, t, :], rt_o[:, t, :], rt_rs[:, :], ALU.mult).then_inc(*own.sig())
                    dve.wait_ge(rel["act"], PLAN.released(u0 + 6 * g + 4 + hh)[1])
                    for t in range(2):
                        mine()
                        V.scalar_tensor_tensor(rt_o[:, t, :], rt_o[:, t, :], col("gnw", 2 * hd + t), rt_g[:, hh, t, :], ALU.mult, ALU.mult)\
                            .then_inc(*own.sig(M("z_ret") if t else None))
                    low_part(xl[:, 2 * hd:2 * hd + 2, :], rt_o[:, :, :], xh[:, 2 * hd:2 * hd + 2, :], xl_ready, xh_ready, 4 * X_GEN["ret"] + hd + 1)
            s0, u0 = PLAN.at["reto"]
            for j in range(4):
                dve.wait_ge(rel["act"], PLAN.released(PLAN.at["gret"][1] + j)[1])
                done(u0 + j)
                V.tensor_tensor(mixt[:, 2 * j:2 * j + 2, :], sgt[:, 2 * j:2 * j + 2, :], banks(u0 + j), ALU.mult).then_inc(*own.sig(rel["dve"]))
            s0, u0 = PLAN.at["xlru"]
            for j in range(4):
                dve.wait_ge(M("tap"), 2 * j + 2)
                for t in range(2):
                    k = 2 * j + t
                    for b in (1, 2, 3):
                        mine()
                        V.scalar_tensor_tensor(xc[:, k, b:S], banks(u0 + j)[:, t, 0:S - b], col("lconvw", 8 * (3 - b) + k), xc[:, k, b:S], ALU.mult, ALU.add)\
                            .then_inc(*own.sig(rel["dve"] if t and b == 3 else None))
                p2 = slice(2 * j, 2 * j + 2)
                low_part(xl[:, p2, :], xc[:, p2, :], xh[:, p2, :], xl_ready, xh_ready, 4 * X_GEN["conv"] + j + 1)
            s0, u0 = PLAN.at["lru"]
            for n in range(4):
                p2 = slice(2 * n, 2 * n + 2)
                dve.wait_ge(rel["act"], PLAN.released(u0 + 3 * n + 2)[1])
                mine()
                V.tensor_tensor(xc[:, p2, :], xc[:, p2, :], li[:, :, :], ALU.mult).then_inc(*own.sig())
                dve.wait_ge(M("u_act"), 2 * n + 2)
                mine()
                V.tensor_tensor(li[:, :, :], la[:, :, :], la[:, :, :], ALU.mult).then_inc(*own.sig(M("b_done")))
                mine()
                V.scalar_tensor_tensor(lu[:, :, :], li[:, :, :], 1.0, lu[:, :, :], ALU.add, ALU.mult).then_inc(*own.sig(M("b_done")))
                dve.wait_ge(M("r_act"), n + 1)
                V.tensor_tensor(xc[:, p2, :], xc[:, p2, :], lu[:, :, :], ALU.mult).then_inc(*own.sig(M("b_done")))
                mine()
                for t in range(2):
                    V.tensor_tensor_scan(xc[:, 2 * n + t, :], la[:, t, :], xc[:, 2 * n + t, :], 0.0, ALU.mult, ALU.add).then_inc(*own.sig(M("hl_done")))
            s0, u0 = PLAN.at["ylru"]
            for j in range(4):
                p2 = slice(2 * j, 2 * j + 2)
                dve.wait_ge(rel["act"], PLAN.released(u0 + j)[1])
                mine()
                V.tensor_tensor(lr[:, :, :], lr[:, :, :], xc[:, p2, :], ALU.mult).then_inc(*own.sig(M("z_lru")))
                low_part(xl[:, p2, :], lr[:, :, :], xh[:, p2, :], xl_ready, xh_ready, 4 * X_GEN["lru"] + j + 1)
            s0, u0 = PLAN.at["lruo"]
            for j in range(4):
                p2 = slice(2 * j, 2 * j + 2)
                dve.wait_ge(rel["act"], PLAN.released(PLAN.at["lru"][1] + 3 * j)[1])
                done(u0 + j)
                V.tensor_tensor(sgt[:, p2, :], sgt[:, p2, :], banks(u0 + j), ALU.mult).then_inc(*own.sig(rel["dve"]))
                mine()
                V.tensor_tensor(mixt[:, p2, :], mixt[:, p2, :], sgt[:, p2, :], ALU.add).then_inc(*own.sig(M("mixed")))
                low_part(gl[:, p2, :], mixt[:, p2, :], gh[:, p2, :], gl_ready, gh_ready, 4 * G_GEN["mixed"] + j + 1)
            s0, u0 = PLAN.at["wout"]
            for j in range(4):
                add_unit(u0 + j, j)
                sums(j, 9, with_mean=False)
            rms_apply(9, "norm2", xh, xl, xl_ready)
            s0, u0 = PLAN.at["ffnb"]
            g0 = 4 * G_GEN["ffnb"]

            def third(q):
                for j in range(4):
                    dve.wait_ge(M("tap2"), q * 8 + (2 * j + 2) if q is not None else 16 + 2 * j + 2)
                    for t in range(2):
                        k = 2 * j + t
                        for b in (1, 2):
                            w = vec[:, bass.ds(q * 8 + (VEC["fconvw"] + 24 * (2 - b) + k), 1)] if q is not None else col("fconvw", 24 * (2 - b) + 16 + k)
                            if own.at is not None:
                                mine()
                            V.scalar_tensor_tensor(cv[:, t, b:S], banks(u0 + 2 * j)[:, t, 0:S - b], w, cv[:, t, b:S], ALU.mult, ALU.add)\
                                .then_inc(*own.sig(rel["dve"] if t and b == 2 else None))
                    dve.wait_ge(M("gelu2"), q * 4 + (j + 1) if q is not None else 8 + j + 1)
                    dve.wait_ge(unit_done, q * 12 + (u0 + 2 * j + 2) if q is not None else u0 + 2 * j + 26)
                    mine()
                    V.tensor_tensor(hid2[:, :, :], cv[:, :, :], banks(u0 + 2 * j + 1), ALU.mult).then_inc(*own.sig(rel["dve"]))
                    dve.wait_ge(gh_ready, q * 4 + (g0 + j + 1) if q is not None else g0 + 8 + j + 1)
                    V.tensor_tensor(gl[:, 2 * j:2 * j + 2, :], hid2[:, :, :], gh[:, 2 * j:2 * j + 2, :].bitcast(F32), ALU.subtract)\
                        .then_inc(*own.sig(gl_ready))
                for j in range(4):
                    p2 = slice(2 * j, 2 * j + 2)
                    dve.wait_ge(unit_done, q * 12 + (u0 + 8 + j + 1) if q is not None else u0 + 33 + j)
                    mine()
                    V.tensor_tensor(h[:, p2, :], h[:, p2, :], banks(u0 + 8 + j), ALU.add).then_inc(*own.sig(rel["dve"]))
                    if q is None:
                        sums(j, 10, with_mean=False)

            mine()
            with dve.Fori(0, 2) as q:
                own.enter(q, {rel["dve"]: 12, gl_ready: 4, dve_own: 12})
                third(q)
                mine()
                own.leave(2)
            third(None)
            rms_apply(10, "normf", None, None, None)


LOADS = 7


def sw_blocks(n):
    return min(n, 1) + 1


def sw_q_index(k, kb):
    return 7 * (k // 4) + max(2 * (k % 4) - 1, 0) + kb


def post_base(layer):
    return {0: 0, 1: 8, 3: 16}[layer]



_ORDER = ["stream", "x", "p", "positions", "vectors", "rel_bias", "onehot", "eye", "swap", "picks", "decay", "resets"]


def constants():
    f = np.float32
    y = np.arange(640)
    n = 511 - y
    nn = np.maximum(n, 0)
    exact = N_BUCKETS // 2
    large = exact + np.floor(np.log(np.maximum(nn, 1) / exact) / math.log(MAX_DISTANCE / exact) * (N_BUCKETS - exact) + 1e-9)
    bucket = np.where(nn < exact, nn, np.minimum(large, N_BUCKETS - 1)).astype(int)
    onehot = np.zeros((33, 1280), f)
    for half in range(2):
        onehot[bucket, half * 640 + y] = 1.0
    onehot[32, 0:640] = np.where(n < 0, NEG, 0.0)
    onehot[32, 640:1280] = np.where((n < 0) | (n >= P), NEG, 0.0)
    eye = np.eye(P, dtype=f)
    swap = np.zeros((P, P), f)
    for i in range(64):
        swap[i + 64, i] = -1.0
        swap[i, i + 64] = 1.0
    s, t = np.arange(P)[:, None], np.arange(P)[None, :]
    picks = np.stack([((s // (2 * b) == t // (2 * b)) & (s % (2 * b) < b) & (t % (2 * b) >= b)).astype(np.int32)
                      for b in HG_LEVELS], 1)
    j, i = np.arange(P)[:, None], np.arange(S)[None, :]
    same = i // 64 == j // 64
    dist = np.where(same, np.abs(i - j), np.maximum(i - j, 0)).astype(np.float64)
    keep = same | (i // 64 > j // 64)
    decay = np.stack([np.where(keep, np.exp(np.log1p(-2.0 ** (-5.0 - hd)) * dist), 0.0) for hd in range(RET_HEADS)], 1).astype(f)
    resets = np.broadcast_to((np.arange(S) % P != 0).astype(f), (P, S))
    return onehot, eye, swap, picks, decay, resets


def vectors(inp):
    f = np.float32
    v = np.zeros((P, NVEC), f)

    def put(name, a, at=0):
        a = np.asarray(a, f)
        rows = a.reshape(-1, P) if a.size % P == 0 else None
        v[:, VEC[name] + at:VEC[name] + at + rows.shape[0]] = rows.T

    put("ln_g", inp["ln_g"])
    put("ln_b", inp["ln_b"])
    put("lb", inp["hg_lower_bound"])
    put("gnorm", inp["hg_gnorm"])
    put("subln", inp["da_subln"])
    v[0:64, VEC["lam"]:VEC["lam"] + 8] = np.asarray(inp["da_lambda"], f).reshape(8, 64).T
    v[:, VEC["sinks"]:VEC["sinks"] + 16] = np.asarray(inp["sw_sinks"], f).reshape(1, 16)
    for name, key in (("norm1", "norm1_w_2"), ("mgb", "merge_gate_b_2"), ("gnw", "ret_gn_w_2"), ("lconvw", "lru_conv_w_2"),
                      ("lconvb", "lru_conv_b_2"), ("br", "lru_b_r_2"), ("bi", "lru_b_i_2"), ("lamb", "lru_lambda_2"),
                      ("norm2", "norm2_w_2"), ("fconvw", "ffn_conv_w_2"), ("fconvb", "ffn_conv_b_2"), ("normf", "norm_f_w_2")):
        put(name, inp[key])
    half = 64
    freq = (10000.0 ** (-np.arange(half, dtype=np.float64) / half)).astype(f)
    v[:, VEC["invf"]] = np.concatenate([freq, freq])
    return v


def slab_stream(inp):
    out = np.empty((N_SLABS, P, 2048), np.float32)
    for i, (name, j, k0, c0) in enumerate(PLAN.slabs):
        w = np.asarray(inp[name])[j]
        if k0 == -1:
            out[i] = w.reshape(2, P, 4, 256).transpose(1, 2, 0, 3).reshape(P, 2048)
        elif k0 == -2:
            both = np.stack([w, np.asarray(inp["lru_w_i_2"])[j]])[:, 2 * c0:2 * c0 + 2]
            out[i] = both.reshape(2, 2, 2, P, 256).transpose(3, 1, 0, 2, 4).reshape(P, 2048)
        else:
            out[i] = w[k0:k0 + D, c0:c0 + 256].reshape(KT, P, 256).transpose(1, 0, 2).reshape(P, 2048)
    return out


def features_first(a):
    return np.ascontiguousarray(a.reshape(S, -1, P).transpose(2, 1, 0))


def kernel(**inputs):
    import concourse.bacc as bacc
    from concourse.bass_utils import run_bass_kernel_spmd

    onehot, eye, swap, picks, decay, resets = constants()
    p = np.asarray(inputs["p"])
    arrays = {
        "stream": slab_stream(inputs),
        "x": features_first(np.asarray(inputs["x"])[0]),
        "p": np.stack([features_first(p[i, 0]) for i in range(NL)]),
        "positions": np.ascontiguousarray(np.broadcast_to(np.asarray(inputs["positions_2"]), (P, S))),
        "vectors": vectors(inputs),
        "rel_bias": np.ascontiguousarray(inputs["rel_bias"]),
        "onehot": onehot, "eye": eye, "swap": swap, "picks": np.ascontiguousarray(picks),
        "decay": np.ascontiguousarray(decay), "resets": np.ascontiguousarray(resets),
    }
    nc = bacc.Bacc("TRN2", target_bir_lowering=False, num_devices=1)
    args = [nc.dram_tensor(f"in_{n}", arrays[n].shape, mybir.dt.from_np(arrays[n].dtype), kind="ExternalInput").ap() for n in _ORDER]
    out = nc.dram_tensor("out_features", (P, KT, S), F32, kind="ExternalOutput").ap()
    build(nc, *args, out)
    r = run_bass_kernel_spmd(nc, [{f"in_{n}": arrays[n] for n in _ORDER}], core_ids=[0])
    got = np.asarray(r.results[0]["out_features"])
    return np.ascontiguousarray(got.transpose(2, 1, 0).reshape(1, S, D))
```
